# Optimizing a Trainium2 kernel written in Bass

```python
import jax, jax.numpy as jnp
from jax import lax
import numpy as np

D_MODEL = 2048
BATCH = 1
SEQ = 256
DEPTH = 1

CHUNK = 64
WINDOW = 128
WINDOW_CHUNKS = WINDOW // CHUNK

ATTN_HEADS = 16
ATTN_KV_HEADS = 4
ATTN_HEAD_DIM = 64
ATTN_GROUP = ATTN_HEADS // ATTN_KV_HEADS
ATTN_WIDTH = ATTN_HEADS * ATTN_HEAD_DIM
KV_WIDTH = ATTN_KV_HEADS * ATTN_HEAD_DIM

HGRN_HEADS = 8
HGRN_KEY_DIM = 128
HGRN_VAL_DIM = 128
HGRN_KEY_WIDTH = HGRN_HEADS * HGRN_KEY_DIM
HGRN_VAL_WIDTH = HGRN_HEADS * HGRN_VAL_DIM

MIX_WIDTH = ATTN_WIDTH + HGRN_VAL_WIDTH
IN_PROJ_WIDTH = ATTN_WIDTH + 2 * KV_WIDTH + 2 * HGRN_KEY_WIDTH + 2 * HGRN_VAL_WIDTH
D_FF = 4 * D_MODEL
EPS = 1e-6

kernel_name = 'hymba_swa_sink_hgrn2_sqrelu_block'

def rms_norm(x, gain):
    x32 = x.astype(jnp.float32)
    y = x32 * lax.rsqrt(jnp.mean(x32 * x32, axis=-1, keepdims=True) + EPS)
    return (y * gain.astype(jnp.float32)).astype(x.dtype)

def layer_lower_bounds(lb_logits):
    p = jax.nn.softmax(lb_logits.astype(jnp.float32), axis=0)
    return jnp.cumsum(p, axis=0)[:DEPTH]

def _shift_chunks(t, j):
    if j == 0:
        return t
    nc = t.shape[1]
    pad = [(0, 0)] * t.ndim
    pad[1] = (j, 0)
    return jnp.pad(t[:, :nc - j], pad)

def sliding_window_sink_attention(q, k, v, sinks):
    B, S = q.shape[0], q.shape[1]
    nc = S // CHUNK
    qc = q.reshape(B, nc, CHUNK, ATTN_KV_HEADS, ATTN_GROUP, ATTN_HEAD_DIM)
    kc = k.reshape(B, nc, CHUNK, ATTN_KV_HEADS, ATTN_HEAD_DIM)
    vc = v.reshape(B, nc, CHUNK, ATTN_KV_HEADS, ATTN_HEAD_DIM)
    offsets = list(range(WINDOW_CHUNKS - 1, -1, -1))
    kb = jnp.concatenate([_shift_chunks(kc, j) for j in offsets], axis=2)
    vb = jnp.concatenate([_shift_chunks(vc, j) for j in offsets], axis=2)
    scale = ATTN_HEAD_DIM ** -0.5
    scores = jnp.einsum('bnqkgd,bnskd->bnkgqs', qc, kb).astype(jnp.float32) * scale
    key_offset = jnp.repeat(jnp.array(offsets, dtype=jnp.int32), CHUNK)
    valid = jnp.arange(nc, dtype=jnp.int32)[:, None] >= key_offset[None, :]
    scores = jnp.where(valid[None, :, None, None, None, :], scores, -jnp.inf)
    sink = sinks.astype(jnp.float32).reshape(ATTN_KV_HEADS, ATTN_GROUP)[None, None, :, :, None, None]
    sink = jnp.broadcast_to(sink, scores.shape[:-1] + (1,))
    probs = jax.nn.softmax(jnp.concatenate([scores, sink], axis=-1), axis=-1)[..., :-1]
    out = jnp.einsum('bnkgqs,bnskd->bnqkgd', probs.astype(v.dtype), vb)
    return out.reshape(B, S, ATTN_WIDTH)

def hgrn2_recurrence(q, f_logit, i, g, lower_bound, norm_gain):
    B, S = q.shape[0], q.shape[1]
    nc = S // CHUNK
    f = lower_bound + (1.0 - lower_bound) * jax.nn.sigmoid(f_logit.astype(jnp.float32))
    log_f = jnp.log(f)
    k = 1.0 - f
    qa = jax.nn.silu(q.astype(jnp.float32))
    iv = i.astype(jnp.float32)

    def to_chunks(t, d):
        return t.reshape(B, nc, CHUNK, HGRN_HEADS, d).transpose(1, 0, 3, 2, 4)

    causal = jnp.tril(jnp.ones((CHUNK, CHUNK), dtype=bool))[:, :, None]

    def step(state, xs):
        q_c, k_c, v_c, lf_c = xs
        b = jnp.cumsum(lf_c, axis=2)
        diff = b[:, :, :, None, :] - b[:, :, None, :, :]
        decay = jnp.where(causal, jnp.exp(jnp.minimum(diff, 0.0)), 0.0)
        scores = jnp.einsum('bhtsd,bhtd,bhsd->bhts', decay, q_c, k_c)
        o = jnp.einsum('bhts,bhse->bhte', scores, v_c) \
            + jnp.einsum('bhtd,bhde->bhte', q_c * jnp.exp(b), state)
        b_last = b[:, :, -1:, :]
        new_state = jnp.exp(b_last[:, :, 0, :])[..., None] * state \
            + jnp.einsum('bhsd,bhse->bhde', k_c * jnp.exp(b_last - b), v_c)
        return new_state, o

    state0 = jnp.zeros((B, HGRN_HEADS, HGRN_KEY_DIM, HGRN_VAL_DIM), jnp.float32)
    _, o = lax.scan(step, state0, (to_chunks(qa, HGRN_KEY_DIM), to_chunks(k, HGRN_KEY_DIM),
                                  to_chunks(iv, HGRN_VAL_DIM), to_chunks(log_f, HGRN_KEY_DIM)))
    o = o.transpose(1, 0, 3, 2, 4).reshape(B, S, HGRN_HEADS, HGRN_VAL_DIM)
    o = o * lax.rsqrt(jnp.mean(o * o, axis=-1, keepdims=True) + EPS)
    o = o.reshape(B, S, HGRN_VAL_WIDTH) * norm_gain.astype(jnp.float32)
    o = o * jax.nn.silu(g.astype(jnp.float32))
    return o.astype(q.dtype)

def setup_inputs(seed: int = 0) -> dict:
    key = jax.random.key(seed)
    ks = jax.random.split(key, 11)
    f32 = jnp.float32
    x = jax.random.normal(ks[0], (BATCH, SEQ, D_MODEL), f32)
    norm_mix = 1.0 + 0.02 * jax.random.normal(ks[1], (DEPTH, D_MODEL), f32)
    w_in = jax.random.normal(ks[2], (DEPTH, D_MODEL, IN_PROJ_WIDTH), f32) * D_MODEL ** -0.5
    attn_sinks = 0.5 * jax.random.normal(ks[3], (DEPTH, ATTN_HEADS), f32)
    lb_logits = 0.1 * jax.random.normal(ks[4], (DEPTH + 1, HGRN_KEY_WIDTH), f32)
    hgrn_norm = 1.0 + 0.02 * jax.random.normal(ks[5], (DEPTH, HGRN_VAL_WIDTH), f32)
    w_out = jax.random.normal(ks[6], (DEPTH, MIX_WIDTH, D_MODEL), f32) * MIX_WIDTH ** -0.5
    norm_mlp = 1.0 + 0.02 * jax.random.normal(ks[7], (DEPTH, D_MODEL), f32)
    w_up = jax.random.normal(ks[8], (DEPTH, D_MODEL, D_FF), f32) * D_MODEL ** -0.5
    w_down = jax.random.normal(ks[9], (DEPTH, D_FF, D_MODEL), f32) * D_FF ** -0.5
    final_norm = 1.0 + 0.02 * jax.random.normal(ks[10], (D_MODEL,), f32)
    return {'x': x, 'norm_mix': norm_mix, 'w_in': w_in, 'attn_sinks': attn_sinks,
            'lb_logits': lb_logits, 'hgrn_norm': hgrn_norm, 'w_out': w_out,
            'norm_mlp': norm_mlp, 'w_up': w_up, 'w_down': w_down, 'final_norm': final_norm}

def reference(x, norm_mix, w_in, attn_sinks, lb_logits, hgrn_norm, w_out,
              norm_mlp, w_up, w_down, final_norm):
    lower_bounds = layer_lower_bounds(lb_logits)
    split_points = np.cumsum([ATTN_WIDTH, KV_WIDTH, KV_WIDTH, HGRN_KEY_WIDTH,
                              HGRN_KEY_WIDTH, HGRN_VAL_WIDTH])
    h = x
    for l in range(DEPTH):
        u = rms_norm(h, norm_mix[l])
        proj = jnp.einsum('bsd,de->bse', u, w_in[l])
        q_a, k_a, v_a, q_h, f_h, i_h, g_h = jnp.split(proj, split_points, axis=-1)
        a = sliding_window_sink_attention(q_a, k_a, v_a, attn_sinks[l])
        r = hgrn2_recurrence(q_h, f_h, i_h, g_h, lower_bounds[l], hgrn_norm[l])
        mixed = jnp.concatenate([a, r], axis=-1)
        h = h + jnp.einsum('bse,ed->bsd', mixed, w_out[l])
        v = rms_norm(h, norm_mlp[l])
        hidden = jnp.square(jax.nn.relu(jnp.einsum('bsd,df->bsf', v, w_up[l])))
        h = h + jnp.einsum('bsf,fd->bsd', hidden, w_down[l])
    return rms_norm(h, final_norm)


_drawn_inputs = setup_inputs


def setup_inputs(seed=0):
    import zlib

    import numpy as np

    out = dict(_drawn_inputs(seed))
    spreads = {}
    factors = {'norm_mix': 4.235,
     'attn_sinks': 64.0,
     'lb_logits': 8.0,
     'hgrn_norm': 6.474,
     'norm_mlp': 11.564,
     'final_norm': 8.233}
    for name, (base, spread) in spreads.items():
        noise = np.random.default_rng([zlib.crc32(name.encode()), seed]).standard_normal(out[name].shape)
        drawn = base * np.exp(spread * noise) if base else spread * noise
        out[name] = __import__('jax').numpy.asarray(drawn.astype(out[name].dtype))
    for name, factor in factors.items():
        out[name] = (out[name] * factor).astype(out[name].dtype)
    return out
```

```python
from contextlib import ExitStack

import concourse.bass as bass
from concourse import mybir

F32 = mybir.dt.float32
F32R = mybir.dt.float32r
U8 = mybir.dt.uint8
ACT = mybir.ActivationFunctionType
ALU = mybir.AluOpType
AX = mybir.AxisListType

P = 128
D_MODEL = 2048
SEQ = 256
KT = D_MODEL // P
COLS = 256
UNITS = 4
UK = KT // UNITS
D_FF = 4 * D_MODEL
CHUNKS = D_FF // D_MODEL
N_GROUPS = D_MODEL // COLS
HEAD_DIM = 64
HEADS = 16
KV_HEADS = 4
CHUNK = 64
N_CHUNKS = SEQ // CHUNK
H_HEADS = 8
LEVELS = 8
SCALE = HEAD_DIM ** -0.5
EPS = 1e-6

Q_A, K_A, V_A, Q_H, F_H, I_H, G_H = 0, 4, 5, 6, 10, 14, 18
ITERS = 4
G_K, G_V, G_QA, G_HG, G_OUT, G_MLP = 0, 1, 2, 6, 22, 30
G_END = G_MLP + CHUNKS * 2 * N_GROUPS

C_MIX, C_MLP, C_FIN, C_HG, C_LB = 0, 16, 32, 48, 56
C_ALL = 72


def build(nc, x, norm_mix, w_in, attn_sinks, lb_logits, hgrn_norm, w_out, norm_mlp, w_up, w_down,
          final_norm, identity, level_masks, out):
    with ExitStack() as ctx:
        def sb(name, shape, dt=F32):
            return ctx.enter_context(nc.sbuf_tensor(name, shape, dt))

        def sem(name):
            return ctx.enter_context(nc.semaphore(name))

        ps = ctx.enter_context(nc.psum_tensor("ps", [P, 8, 512], F32))

        raw = sb("raw", [P, UNITS, UK, COLS])
        w_hi = sb("w_hi", [P, 2 * UNITS, UK, COLS], F32R)
        w_lo = sb("w_lo", [P, 2 * UNITS, UK, COLS], F32R)
        act_in = sb("act_in", [P, KT, 2 * SEQ], F32R)
        act_mid = sb("act_mid", [P, KT, 2 * SEQ], F32R)
        resid = sb("resid", [P, KT, SEQ])
        qa_t = sb("qa_t", [P, 8, SEQ])
        k_dup = sb("k_dup", [P, KV_HEADS, SEQ])
        v_all = sb("v_all", [P, 3, COLS])
        q_st = sb("q_st", [P, 2, SEQ])
        k_st = sb("k_st", [P, SEQ])
        v_st = sb("v_st", [P, 3, HEAD_DIM])
        lb_st = sb("lb_st", [P, 2, 2])
        gain_st = sb("gain_st", [P, 2])
        sink_st = sb("sink_st", [P, 2, 2])
        half = sb("half", [P, 2, 2, SEQ])
        big = sb("big", [P, 4, 512])
        hg = sb("hg", [P, 4, 512])
        sig = hg[:, 1, :]
        i_nat = sb("i_nat", [P, 2, COLS])
        s_t = sb("s_t", [P, 4, P])
        s_x = sb("s_x", [P, 2, P])
        ident = sb("ident", [P, P])
        masks = sb("masks", [P, LEVELS, P], U8)
        ones = sb("ones", [P, P])
        cols = sb("cols", [P, C_ALL])
        lbc = sb("lbc", [P, 2, H_HEADS])
        lbe = sb("lbe", [P, 4, H_HEADS])
        sinks_b = sb("sinks_b", [P, HEADS])
        sink_c = sb("sink_c", [P, 2, 8])
        eps_c = sb("eps_c", [P, 1])
        stat = sb("stat", [P, 8])
        wait_mark = sb("wait_mark", [P, LEVELS])
        amax = sb("amax", [P, 2, 4])
        negm = sb("negm", [P, 2, 4])
        asum = sb("asum", [P, 2, 4])
        esink = sb("esink", [P, 2, 4])
        rstd = sb("rstd", [P, SEQ])

        x_nat = [qa_t[:, :, :].rearrange("p a b -> p (a b)"), big[:, :, :].rearrange("p a b -> p (a b)")]
        mask_f = half[:, :, :, :].rearrange("p a b c -> p (a b c)").rearrange("p (l t) -> p l t", l=LEVELS)
        prm = i_nat[:, 0, 0:P]
        k_t = i_nat
        sq_acc = hg[:, 0, :].rearrange("p (a b) -> p a b", a=2)
        D, U, KK, QS = (hg[:, n, :] for n in range(4))
        probs = [big[:, c, :].rearrange("p (n k) -> p n k", n=4) for c in range(2)]
        probs_t = [big[:, 2 + c, :].rearrange("p (n k) -> p n k", n=4) for c in range(2)]
        U0 = big[:, :, :].rearrange("p a b -> p (a b)")
        stage4 = [U0[:, 1024 * n:1024 * n + 1024].rearrange("p (a b) -> p a b", a=4) for n in range(2)]
        relu_b = [big[:, n, :].rearrange("p (a b) -> p a b", a=2) for n in range(2)]
        sq_b = [big[:, 2 + n, :].rearrange("p (a b) -> p a b", a=2) for n in range(2)]
        y_nat = raw[:, :, :, :].rearrange("p a b c -> p (a b c)")

        raw_landed = [sem(f"raw_landed{n}") for n in range(UNITS)]
        x_landed = [sem("x_landed0"), sem("x_landed1")]
        prm_landed = sem("prm_landed")
        const_landed = sem("const_landed")
        masks_landed = sem("masks_landed")
        sinks_landed = sem("sinks_landed")
        consts_set = sem("consts_set")
        hi_ready = sem("hi_ready")
        lo_ready = sem("lo_ready")
        unit_used = sem("unit_used")
        half_copied = sem("half_copied")
        acc_free = sem("acc_free")
        dve_step = sem("dve_step")
        act_step = sem("act_step")
        cols_turned = sem("cols_turned")
        cols_ready = sem("cols_ready")
        lb_shifted = sem("lb_shifted")
        lb_exp = sem("lb_exp")
        x_turned = sem("x_turned")
        resid_a = sem("resid_a")
        resid_v = sem("resid_v")
        std_ready = sem("std_ready")
        diag_ready = sem("diag_ready")
        rstd_spread = sem("rstd_spread")
        norm_ready = sem("norm_ready")
        in_hi = sem("in_hi")
        in_ready = sem("in_ready")
        kt_ready = sem("kt_ready")
        k_dup_landed = sem("k_dup_landed")
        staged = sem("staged")
        scores_ready = sem("scores_ready")
        negm_ready = sem("negm_ready")
        exp_ready = sem("exp_ready")
        probs_ready = sem("probs_ready")
        probs_turned = sem("probs_turned")
        probs_copied = sem("probs_copied")
        att_ready = sem("att_ready")
        att_hi = sem("att_hi")
        att_mixed = sem("att_mixed")
        sig_ready = sem("sig_ready")
        gates_ready = sem("gates_ready")
        level_ready = sem("level_ready")
        level_done = sem("level_done")
        level_taken = sem("level_taken")
        cross_copied = sem("cross_copied")
        o_ready = sem("o_ready")
        osq_ready = sem("osq_ready")
        oms_ready = sem("oms_ready")
        ostd_ready = sem("ostd_ready")
        o_scaled = sem("o_scaled")
        hg_hi = sem("hg_hi")
        hg_mixed = sem("hg_mixed")
        resid_ready = sem("resid_ready")
        scaled_ready = sem("scaled_ready")
        sq_ready = sem("sq_ready")
        v_hi = sem("v_hi")
        v_ready = sem("v_ready")
        sq_summed = sem("sq_summed")
        ms_ready = sem("ms_ready")
        ms_half = sem("ms_half")
        ms_sum = sem("ms_sum")
        mstd_ready = sem("mstd_ready")
        relu_ready = sem("relu_ready")
        hid_sq = sem("hid_sq")
        hid_hi = sem("hid_hi")
        hid_ready = sem("hid_ready")
        fin_sq = sem("fin_sq")
        fin_gained = sem("fin_gained")
        fin_summed = sem("fin_summed")
        fms_ready = sem("fms_ready")
        fstd_ready = sem("fstd_ready")
        frstd_ready = sem("frstd_ready")
        y_turned = sem("y_turned")
        y_a = sem("y_a")
        y_v = sem("y_v")
        y_stored = sem("y_stored")
        dve_done_resid = sem("resid_done")
        mlp_rstd = sem("mlp_rstd")
        fin_total = sem("fin_total")

        block = ctx.enter_context(nc.Block())

        def bank_pair(par):
            return ps[:, 2 * par:2 * par + 2, :]

        @block.sync
        def _(sp):
            def load(g, par, src, row0, col0, first=False):
                for u in range(UNITS):
                    if not first:
                        sp.wait_ge(lo_ready, g * UNITS + (u - UNITS + 1))
                    rows = row0 + u * UK * P
                    sp.dma_start(
                        raw[:, u, :, :],
                        src[0, bass.ds(rows, UK * P), bass.ds(col0, COLS)].rearrange("(k p) n -> p k n", p=P),
                    ).then_inc(raw_landed[u], 16)

            for st in range(2):
                sp.dma_start(x_nat[st], x[0, st * P:(st + 1) * P, :]).then_inc(x_landed[st], 16)
            load(G_K, 0, w_in, 0, K_A * COLS, first=True)
            load(G_V, 1, w_in, 0, V_A * COLS)
            with sp.Fori(0, 2) as it:
                for j in range(2):
                    load(it * 2 + (G_QA + j), j, w_in, 0, it * (2 * COLS) + (Q_A + j) * COLS)
            with sp.Fori(0, ITERS) as it:
                for j, part in enumerate((F_H, Q_H, I_H, G_H)):
                    load(it * 4 + (G_HG + j), j % 2, w_in, 0, it * COLS + part * COLS)
            with sp.Fori(0, N_GROUPS // 2) as it:
                for j in range(2):
                    load(it * 2 + (G_OUT + j), j, w_out, 0, it * (2 * COLS) + j * COLS)
            with sp.Fori(0, CHUNKS) as c:
                with sp.Fori(0, N_GROUPS // 2) as it:
                    for j in range(2):
                        load(c * (2 * N_GROUPS) + it * 2 + (G_MLP + j), j, w_up, 0,
                             c * D_MODEL + it * (2 * COLS) + j * COLS)
                with sp.Fori(0, N_GROUPS // 2) as it:
                    for j in range(2):
                        load(c * (2 * N_GROUPS) + it * 2 + (G_MLP + N_GROUPS + j), j, w_down, c * D_MODEL,
                             it * (2 * COLS) + j * COLS)
            for n in range(4):
                for st, ready in ((0, y_a), (1, y_v)):
                    sp.wait_ge(ready, n + 1)
                    sp.dma_start(out[0, st * P:(st + 1) * P, 512 * n:512 * n + 512],
                                 y_nat[:, st * D_MODEL + 512 * n:st * D_MODEL + 512 * n + 512],
                                 ).then_inc(y_stored, 16)
            sp.wait_ge(y_stored, 8 * 16)

        @block.gpsimd
        def _(pool):
            nc.gpsimd.memset(ones[:, :], 1.0).then_inc(consts_set, 1)
            nc.gpsimd.memset(eps_c[:, :], EPS).then_inc(consts_set, 1)
            nc.gpsimd.memset(s_t[:, :, :], 0.0).then_inc(consts_set, 1)

        CONSTS = 3

        @block.scalar
        def _(act):
            def split(g, par, u, first=False):
                act.wait_ge(raw_landed[u], g * 16 + 16)
                if not first:
                    act.wait_ge(unit_used, g * UNITS + (u + 1 - 2 * UNITS))
                nc.scalar.activation(w_hi[:, par * UNITS + u, :, :], raw[:, u, :, :], ACT.Copy).then_inc(hi_ready, 1)

            def copy_half(g, par):
                act.wait_ge(unit_used, g * UNITS + UNITS)
                nc.scalar.activation(half[:, par, :, :], bank_pair(par)[:, :, SEQ:2 * SEQ], ACT.Copy).then_inc(half_copied, 1)

            act.dma_start(ident[:, :], identity[:, :]).then_inc(const_landed, 16)
            for n, (at, src) in enumerate((
                    (C_MIX, norm_mix.rearrange("a (t p) -> (a t) p", p=P)),
                    (C_MLP, norm_mlp.rearrange("a (t p) -> (a t) p", p=P)),
                    (C_FIN, final_norm.rearrange("(t p) -> t p", p=P)),
                    (C_HG, hgrn_norm.rearrange("a (t p) -> (a t) p", p=P)),
                    (C_LB, lb_logits.rearrange("a (t p) -> (a t) p", p=P)))):
                act.dma_start(prm[at:at + src.shape[0], :], src).then_inc(prm_landed, 16)
            act.dma_start(mask_f, level_masks[:, :, :]).then_inc(masks_landed, 16)
            act.dma_start(sinks_b[:, :], attn_sinks[0:1, :].to_broadcast([P, HEADS])).then_inc(sinks_landed, 16)

            act.wait_ge(consts_set, CONSTS)
            for st in range(2):
                act.wait_ge(x_landed[st], 16)
                nc.scalar.activation(hg[:, :, :].rearrange("p a b -> p (a b)"), x_nat[st], ACT.Square,
                                     accum_out=stat[:, st:st + 1]).then_inc(act_step, 1)
                act.wait_ge(act_step, st + 1)
            nc.scalar.activation(stat[:, 2:4], stat[:, 0:2], ACT.Sqrt, bias=eps_c[:, 0:1],
                                 scale=1.0 / D_MODEL).then_inc(std_ready, 1)
            for n in range(4):
                b = 2 * n + 1
                act.wait_ge(x_turned, b + 1)
                nc.scalar.activation(resid[:, 2 * b:2 * b + 2, :], ps[:, b, :].rearrange("p (a b) -> p a b", a=2),
                                     ACT.Copy).then_inc(resid_a, 1)
            for u in range(UNITS):
                act.wait_ge(norm_ready, u + 1)
                nc.scalar.activation(act_in[:, UK * u:UK * u + UK, 0:SEQ], stage4[u % 2], ACT.Copy).then_inc(in_hi, 1)
                split(G_K, 0, u, first=True)
            act.wait_ge(lb_shifted, 1)
            nc.scalar.activation(lbe[:, 2:4, :], lbe[:, 0:2, :], ACT.Exp).then_inc(lb_exp, 1)

            for u in range(UNITS):
                split(G_V, 1, u, first=True)
            copy_half(G_K, 0)
            act.wait_ge(kt_ready, 1)
            for to in range(2):
                for frm in range(2):
                    act.dma_start(k_dup[to * 64:to * 64 + 64, frm::2, :], k_t[frm * 64:frm * 64 + 64, :, :]).then_inc(k_dup_landed, 16)
            for u in range(UNITS):
                split(G_QA, 0, u)
            with act.Fori(0, 2) as it:
                for j in range(2):
                    for u in range(UNITS):
                        split(it * 2 + (G_QA + j + 1), 1 - j, u)
                    copy_half(it * 2 + (G_QA + j), j)

            with act.Fori(0, ITERS) as it:
                g = it * 4 + G_HG

                for u in range(UNITS):
                    split(g + 1, 1, u)
                    if u == 1:
                        for c in range(2):
                            act.wait_ge(negm_ready, it * 2 + (c + 1))
                            for n in range(N_CHUNKS):
                                w = CHUNK if n == 0 else 2 * CHUNK
                                nc.scalar.activation(probs[c][:, n, 0:w], ps[:, 4 + c, n * P:n * P + w], ACT.Exp,
                                                     bias=negm[:, c, n:n + 1], scale=SCALE,
                                                     accum_out=asum[:, c, n:n + 1])
                            nc.scalar.activation(esink[:, c, :], negm[:, c, :], ACT.Exp,
                                                 bias=sink_st[:, 0, c:c + 1]).then_inc(exp_ready, 1)
                copy_half(g, 0)
                act.wait_ge(acc_free, g + 1)
                nc.scalar.activation(sig[:, :], half[:, 0, :, :].rearrange("p a b -> p (a b)"), ACT.Sigmoid).then_inc(sig_ready, 1)

                for u in range(UNITS):
                    split(g + 2, 0, u)
                    if u == 1:
                        for c in range(2):
                            act.wait_ge(probs_turned, it * 2 + (c + 1))
                            nc.scalar.activation(probs_t[c], ps[:, 6 + c, :].rearrange("p (n k) -> p n k", n=4),
                                                 ACT.Copy).then_inc(probs_copied, 1)
                    if u == 3:
                        act.wait_ge(att_ready, it + 1)
                        nc.scalar.activation(act_mid[:, bass.ds(it * 2, 2), 0:SEQ], ps[:, 4:6, 0:SEQ], ACT.Copy).then_inc(att_hi, 1)
                copy_half(g + 1, 1)
                act.wait_ge(acc_free, g + 2)
                act.wait_ge(gates_ready, it * 3 + 1)
                nc.scalar.activation(sig[:, :], half[:, 1, :, :].rearrange("p a b -> p (a b)"), ACT.Sigmoid).then_inc(sig_ready, 1)

                for u in range(UNITS):
                    split(g + 3, 1, u)

                for u in range(UNITS):
                    split(g + 4, 0, u)
                    if u == 1:
                        act.wait_ge(level_done, it * 9 + 9)
                        nc.scalar.activation(s_x[:, :, :], ps[:, 6, 0:2 * P].rearrange("p (h t) -> p h t", h=2),
                                             ACT.Copy).then_inc(cross_copied, 1)
                act.wait_ge(o_ready, it + 1)
                nc.scalar.activation(big[:, 0, :], ps[:, 7, :], ACT.Square).then_inc(osq_ready, 1)
                copy_half(g + 3, 1)
                act.wait_ge(acc_free, g + 4)
                act.wait_ge(gates_ready, it * 3 + 2)
                nc.scalar.activation(sig[:, :], half[:, 1, :, :].rearrange("p a b -> p (a b)"), ACT.Sigmoid).then_inc(sig_ready, 1)
                act.wait_ge(oms_ready, it + 1)
                nc.scalar.activation(big[:, 1, :], ps[:, 6, :], ACT.Sqrt, bias=eps_c[:, 0:1], scale=1.0 / P).then_inc(ostd_ready, 1)
                act.wait_ge(o_scaled, it + 1)
                nc.scalar.activation(act_mid[:, bass.ds(it * 2 + 8, 2), 0:SEQ],
                                     big[:, 3, :].rearrange("p (h t) -> p h t", h=2), ACT.Copy).then_inc(hg_hi, 1)

            with act.Fori(0, N_GROUPS // 2) as it:
                for j in range(2):
                    g = it * 2 + (G_OUT + j)
                    for u in range(UNITS):
                        split(g + 1, 1 - j, u)
                    copy_half(g, j)
                    act.wait_ge(resid_ready, it * 2 + (j + 1))
                    nc.scalar.activation(sq_b[j], resid[:, bass.ds(it * 4 + 2 * j, 2), :], ACT.Square).then_inc(sq_ready, 1)
                    act.wait_ge(scaled_ready, it * 2 + (j + 1))
                    nc.scalar.activation(act_in[:, bass.ds(it * 4 + 2 * j, 2), 0:SEQ], relu_b[j], ACT.Copy).then_inc(v_hi, 1)
            act.wait_ge(ms_ready, 1)
            nc.scalar.activation(sig[:, 0:SEQ], ps[:, 4, SEQ:2 * SEQ], ACT.Copy).then_inc(ms_half, 1)
            act.wait_ge(ms_sum, 1)
            nc.scalar.activation(sig[:, SEQ:2 * SEQ], sig[:, 0:SEQ], ACT.Sqrt, bias=eps_c[:, 0:1],
                                 scale=1.0 / D_MODEL).then_inc(mstd_ready, 1)

            def up_step(g, j, n, k):
                for u in range(UNITS):
                    split(g + 1, 1 - j, u)
                copy_half(g, j)
                act.wait_ge(relu_ready, k + 1)
                nc.scalar.activation(sq_b[j], relu_b[j], ACT.Square).then_inc(hid_sq, 1)
                act.wait_ge(hid_sq, k + 1)
                nc.scalar.activation(act_mid[:, bass.ds(n, 2), 0:SEQ], sq_b[j], ACT.Copy).then_inc(hid_hi, 1)

            def chunk(c, last):
                g0 = c * (2 * N_GROUPS) + G_MLP
                with act.Fori(0, N_GROUPS // 2) as it:
                    for j in range(2):
                        up_step(it * 2 + g0 + j, j, it * 4 + 2 * j, c * N_GROUPS + it * 2 + j)
                with act.Fori(0, N_GROUPS // 2 - last) as it:
                    for j in range(2):
                        g = it * 2 + g0 + (N_GROUPS + j)
                        for u in range(UNITS):
                            split(g + 1, 1 - j, u)
                        copy_half(g, j)
                if last:
                    for u in range(UNITS):
                        split(G_END - 1, 1, u)
                    copy_half(G_END - 2, 0)
                    copy_half(G_END - 1, 1)

            with act.Fori(0, CHUNKS - 1) as c:
                chunk(c, 0)
            chunk(CHUNKS - 1, 1)

            act.wait_ge(acc_free, G_END)
            act.wait_ge(dve_done_resid, 1)
            for n in range(4):
                if n >= 2:
                    act.wait_ge(fin_summed, n - 1)
                nc.scalar.activation(stage4[n % 2], resid[:, 4 * n:4 * n + 4, :], ACT.Square).then_inc(fin_sq, 1)
            act.wait_ge(fms_ready, 1)
            nc.scalar.activation(stat[:, 0:2], ps[:, 0, 0:2], ACT.Sqrt, bias=eps_c[:, 0:1],
                                 scale=1.0 / D_MODEL).then_inc(fstd_ready, 1)
            act.wait_ge(frstd_ready, 1)
            for n in range(4):
                act.wait_ge(y_turned, n + 1)
                nc.scalar.activation(y_nat[:, 512 * n:512 * n + 512], ps[:, [2, 4, 6, 0][n], :], ACT.Copy,
                                     scale=stat[:, 2:3]).then_inc(y_a, 1)

        @block.vector
        def _(dve):
            vec = nc.vector

            def split(g, par, u):
                dve.wait_ge(hi_ready, g * UNITS + (u + 1))
                s = par * UNITS + u
                vec.tensor_tensor(w_lo[:, s, :, :], raw[:, u, :, :], w_hi[:, s, :, :].bitcast(F32),
                                  ALU.subtract).then_inc(lo_ready, 1)

            def sum_half(g, par, halves, to=None):
                dve.wait_ge(half_copied, halves)
                to = half[:, par, :, :] if to is None else to
                vec.tensor_tensor(to, bank_pair(par)[:, :, 0:SEQ], half[:, par, :, :], ALU.add).then_inc(acc_free, 1)

            steps = [0]

            def link(ins, base=None):
                steps[0] += 1
                ins.then_inc(dve_step, 1)
                dve.wait_ge(dve_step, steps[0] if base is None else base + steps[0])

            dve.wait_ge(masks_landed, 16)
            vec.tensor_copy(masks[:, :, :], mask_f)
            dve.wait_ge(cols_turned, 1)
            vec.tensor_copy(cols[:, :], ps[:, 7, 0:C_ALL]).then_inc(cols_ready, 1)
            dve.wait_ge(std_ready, 1)
            dve.wait_ge(const_landed, 16)
            link(vec.reciprocal(stat[:, 4:6], stat[:, 2:4]))
            for st in range(2):
                dg = vec.tensor_scalar(s_x[:, st, :], ident[:, :], stat[:, 4 + st:5 + st], None, ALU.mult)
            dg.then_inc(diag_ready, 1)
            for n in range(4):
                b = 2 * n
                dve.wait_ge(x_turned, b + 1)
                vec.tensor_copy(resid[:, 2 * b:2 * b + 2, :],
                                ps[:, b, :].rearrange("p (a b) -> p a b", a=2)).then_inc(resid_v, 1)
            dve.wait_ge(rstd_spread, 1)
            link(vec.tensor_copy(rstd[:, :], ps[:, 0, 0:SEQ]))
            dve.wait_ge(resid_a, 4)
            dve.wait_ge(resid_v, 4)
            dve.wait_ge(cols_ready, 1)
            for u in range(UNITS):
                if u >= 2:
                    dve.wait_ge(in_ready, u - 1)
                for t in range(UK):
                    kt = UK * u + t
                    nm = vec.scalar_tensor_tensor(out=stage4[u % 2][:, t, :], in0=resid[:, kt, :],
                                                  scalar=cols[:, C_MIX + kt:C_MIX + kt + 1], in1=rstd[:, :],
                                                  op0=ALU.mult, op1=ALU.mult)
                nm.then_inc(norm_ready, 1)
                dve.wait_ge(in_hi, u + 1)
                vec.tensor_tensor(act_in[:, UK * u:UK * u + UK, SEQ:2 * SEQ], stage4[u % 2],
                                  act_in[:, UK * u:UK * u + UK, 0:SEQ].bitcast(F32), ALU.subtract).then_inc(in_ready, 1)
                split(G_K, 0, u)
            l0, l1 = cols[:, C_LB:C_LB + 8], cols[:, C_LB + 8:C_LB + 16]
            link(vec.tensor_tensor(lbe[:, 2, :], l0, l1, ALU.max))
            vec.tensor_tensor(lbe[:, 0, :], l0, lbe[:, 2, :], ALU.subtract)
            vec.tensor_tensor(lbe[:, 1, :], l1, lbe[:, 2, :], ALU.subtract).then_inc(lb_shifted, 1)
            dve.wait_ge(lb_exp, 1)
            link(vec.tensor_tensor(lbe[:, 0, :], lbe[:, 2, :], lbe[:, 3, :], ALU.add))
            link(vec.reciprocal(lbe[:, 1, :], lbe[:, 0, :]))
            link(vec.tensor_tensor(lbc[:, 0, :], lbe[:, 2, :], lbe[:, 1, :], ALU.mult))
            link(vec.tensor_scalar(lbc[:, 1, :], lbc[:, 0, :], -1.0, 1.0, ALU.mult, ALU.add))
            dve.wait_ge(sinks_landed, 16)
            for h in range(2):
                vec.tensor_copy(sink_c[64 * h:64 * h + 64, 0, :], sinks_b[64 * h:64 * h + 64, h::2])
                last = vec.tensor_scalar(sink_c[64 * h:64 * h + 64, 1, :], sinks_b[64 * h:64 * h + 64, h::2], -1.0, None, ALU.mult)
            link(last)

            for u in range(UNITS):
                split(G_V, 1, u)
            dve.wait_ge(half_copied, 1)
            vec.tensor_tensor(k_t[:, :, :], bank_pair(0)[:, :, 0:SEQ], half[:, 0, :, :], ALU.add).then_inc(kt_ready, 1)
            dve.wait_ge(kt_ready, 1)
            vec.tensor_copy(stat[:, 6:7], k_t[:, 0, 0:1]).then_inc(acc_free, 1)
            for u in range(UNITS):
                split(G_QA, 0, u)
            dve.wait_ge(unit_used, (G_V + 1) * UNITS)
            vec.tensor_copy(v_all[:, 0:2, :], bank_pair(1)[:, :, 0:COLS])
            vec.tensor_copy(v_all[0:64, 2, :], ps[0:64, 3, 0:COLS])
            vec.tensor_copy(v_all[64:128, 2, :], ps[64:128, 2, 0:COLS]).then_inc(acc_free, 1)
            with dve.Fori(0, 2) as it:
                for j in range(2):
                    for u in range(UNITS):
                        split(it * 2 + (G_QA + j + 1), 1 - j, u)
                    sum_half(it * 2 + (G_QA + j), j, it * 2 + (j + 2), qa_t[:, bass.ds(it * 4 + 2 * j, 2), :])
            dve.wait_ge(acc_free, G_HG)

            def levels_view(t, n):
                return t.rearrange("p (b two n) -> p b two n", two=2, n=n)

            PER_ITER = 23
            pre = steps[0]
            with dve.Fori(0, ITERS) as it:
                steps[0] = pre
                base = it * PER_ITER
                g = it * 4 + G_HG
                lv = it * 9
                n_e = it * 8

                dve.wait_ge(k_dup_landed, 64)
                vec.tensor_copy(k_st[:, :], k_dup[:, bass.ds(it, 1), :].rearrange("p a b -> p (a b)"))
                vec.tensor_copy(q_st[:, :, :], qa_t[:, bass.ds(it * 2, 2), :])
                vec.tensor_copy(v_st[:, :, :], v_all[:, :, bass.ds(it * HEAD_DIM, HEAD_DIM)])
                vec.tensor_copy(lb_st[:, :, :], lbc[:, :, bass.ds(it * 2, 2)])
                vec.tensor_copy(gain_st[:, :], cols[:, bass.ds(it * 2 + C_HG, 2)])
                vec.tensor_copy(sink_st[:, :, :], sink_c[:, :, bass.ds(it * 2, 2)])
                for c in range(2):
                    last = vec.memset(probs[c][:, 0, CHUNK:2 * CHUNK], 0.0)
                last.then_inc(staged, 1)
                dve.wait_ge(staged, it + 1)
                for u in range(UNITS):
                    split(g + 1, 1, u)
                    if u == 1:
                        for c in range(2):
                            dve.wait_ge(scores_ready, it * 2 + (c + 1))
                            link(vec.tensor_reduce(amax[:, c, :], ps[:, 4 + c, :].rearrange("p (n k) -> p n k", n=4),
                                                   AX.X, ALU.max), base)
                            vec.tensor_scalar(negm[:, c, :], amax[:, c, :], -SCALE, sink_st[:, 1, c:c + 1],
                                              ALU.mult, ALU.min).then_inc(negm_ready, 1)
                for c in range(2):
                    dve.wait_ge(exp_ready, it * 2 + (c + 1))
                    link(vec.tensor_tensor(asum[:, c, :], asum[:, c, :], esink[:, c, :], ALU.add), base)
                    link(vec.reciprocal(esink[:, c, :], asum[:, c, :]), base)
                    vec.tensor_tensor(probs[c], probs[c], esink[:, c, :].unsqueeze(2).to_broadcast([P, 4, P]),
                                      ALU.mult).then_inc(probs_ready, 1)
                sum_half(g, 0, it * 3 + 6)
                dve.wait_ge(sig_ready, it * 3 + 1)
                for h in range(2):
                    sl = slice(h * SEQ, h * SEQ + SEQ)
                    last = vec.tensor_scalar(D[:, sl], sig[:, sl], lb_st[:, 1, h:h + 1], lb_st[:, 0, h:h + 1], ALU.mult, ALU.add)
                last.then_inc(gates_ready, 1)
                dve.wait_ge(gates_ready, it * 3 + 1)
                link(vec.tensor_scalar(KK, D, -1.0, 1.0, ALU.mult, ALU.add), base)

                for u in range(UNITS):
                    split(g + 2, 0, u)
                dve.wait_ge(att_hi, it + 1)
                at = act_mid[:, bass.ds(it * 2, 2), :]
                vec.tensor_tensor(at[:, :, SEQ:2 * SEQ], ps[:, 4:6, 0:SEQ], at[:, :, 0:SEQ].bitcast(F32),
                                  ALU.subtract).then_inc(att_mixed, 1)
                sum_half(g + 1, 1, it * 3 + 7)
                dve.wait_ge(sig_ready, it * 3 + 2)
                dve.wait_ge(acc_free, g + 2)
                vec.tensor_tensor(QS, half[:, 1, :, :].rearrange("p a b -> p (a b)"), sig[:, :], ALU.mult).then_inc(gates_ready, 1)
                dve.wait_ge(gates_ready, it * 3 + 2)

                def operand(l):
                    n = 1 << l
                    E = levels_view(big[:, l % 4, :], n)
                    d, uu, kk, qq = (levels_view(t, n) for t in (D, U, KK, QS))
                    if l >= 4:
                        dve.wait_ge(level_done, lv + (l - 4 + 2))
                    if l == 0:
                        vec.tensor_copy(E[:, :, 0, :], kk[:, :, 0, :])
                    else:
                        vec.tensor_tensor(E[:, :, 0, :], kk[:, :, 0, :], uu[:, :, 0, :], ALU.mult)
                    vec.tensor_tensor(E[:, :, 1, :], qq[:, :, 1, :], d[:, :, 1, :], ALU.mult).then_inc(level_ready, 1)
                    if l == LEVELS - 1:
                        return
                    shape = [P, 512 // (2 * n), n]
                    if l == 0:
                        vec.memset(uu[:, :, 1, :], 1.0)
                        link(vec.tensor_copy(uu[:, :, 0, :], d[:, :, 1, :]), base)
                    else:
                        link(vec.tensor_tensor(uu[:, :, 0, :], uu[:, :, 0, :],
                                               d[:, :, 1, n - 1:n].to_broadcast(shape), ALU.mult), base)
                    link(vec.tensor_tensor(d[:, :, 1, :], d[:, :, 1, :],
                                           d[:, :, 0, n - 1:n].to_broadcast(shape), ALU.mult), base)

                def take(i):
                    dve.wait_ge(level_done, lv + (i + 1))
                    if i:
                        dve.wait_ge(level_taken, it * 8 + i)
                    vec.memset(wait_mark[:, i:i + 1], 0.0)
                    vec.copy_predicated(s_t[:, :, :], masks[:, i:i + 1, :].to_broadcast([P, 4, P]),
                                        ps[:, 4 + i % 2, :].rearrange("p (a b) -> p a b", a=4)).then_inc(level_taken, 1)

                operand(0)
                split(g + 3, 1, 0)
                operand(1)
                operand(2)
                split(g + 3, 1, 1)
                operand(3)
                take(0)
                take(1)
                split(g + 3, 1, 2)
                operand(4)
                take(2)
                take(3)
                operand(5)
                split(g + 3, 1, 3)
                take(4)
                operand(6)
                take(5)
                dve.wait_ge(unit_used, g * UNITS + 3 * UNITS)
                vec.tensor_copy(i_nat[:, :, :], bank_pair(0)[:, :, 0:COLS]).then_inc(acc_free, 1)
                operand(7)

                split(g + 4, 0, 0)
                take(6)
                take(7)
                for u in range(1, UNITS):
                    split(g + 4, 0, u)
                sum_half(g + 3, 1, it * 3 + 8)
                dve.wait_ge(sig_ready, it * 3 + 3)
                dve.wait_ge(acc_free, g + 4)
                for h in range(2):
                    sl = slice(h * SEQ, h * SEQ + SEQ)
                    last = vec.scalar_tensor_tensor(out=QS[:, sl], in0=sig[:, sl], scalar=gain_st[:, h:h + 1],
                                                    in1=half[:, 1, h, :], op0=ALU.mult, op1=ALU.mult)
                last.then_inc(gates_ready, 1)
                dve.wait_ge(ostd_ready, it + 1)
                link(vec.reciprocal(big[:, 2, :], big[:, 1, :]), base)
                dve.wait_ge(gates_ready, it * 3 + 3)
                link(vec.tensor_tensor(big[:, 2, :], big[:, 2, :], QS, ALU.mult), base)
                vec.tensor_tensor(big[:, 3, :], ps[:, 7, :], big[:, 2, :], ALU.mult).then_inc(o_scaled, 1)
                dve.wait_ge(hg_hi, it + 1)
                at = act_mid[:, bass.ds(it * 2 + 8, 2), :]
                vec.tensor_tensor(at[:, :, SEQ:2 * SEQ], big[:, 3, :].rearrange("p (h t) -> p h t", h=2),
                                  at[:, :, 0:SEQ].bitcast(F32), ALU.subtract).then_inc(hg_mixed, 1)
                PER = steps[0] - pre
            assert PER == PER_ITER, PER
            HALVES = 1 + 4 + 3 * ITERS
            after = PER_ITER * ITERS - PER_ITER

            link(vec.memset(sq_acc, 0.0), after)
            with dve.Fori(0, N_GROUPS // 2) as it:
                for j in range(2):
                    g = it * 2 + (G_OUT + j)
                    for u in range(UNITS):
                        split(g + 1, 1 - j, u)
                    sum_half(g, j, it * 2 + (HALVES + j + 1))
                    dve.wait_ge(acc_free, g + 1)
                    tiles = bass.ds(it * 4 + 2 * j, 2)
                    vec.tensor_tensor(resid[:, tiles, :], resid[:, tiles, :], half[:, j, :, :], ALU.add).then_inc(resid_ready, 1)
                    dve.wait_ge(resid_ready, it * 2 + (j + 1))
                    vec.tensor_tensor(relu_b[j], resid[:, tiles, :],
                                      cols[:, bass.ds(it * 4 + (C_MLP + 2 * j), 2)].unsqueeze(2).to_broadcast([P, 2, SEQ]),
                                      ALU.mult).then_inc(scaled_ready, 1)
                    dve.wait_ge(sq_ready, it * 2 + (j + 1))
                    vec.tensor_tensor(sq_acc, sq_acc, sq_b[j], ALU.add).then_inc(sq_summed, 1)
                    dve.wait_ge(v_hi, it * 2 + (j + 1))
                    vec.tensor_tensor(act_in[:, tiles, SEQ:2 * SEQ], relu_b[j], act_in[:, tiles, 0:SEQ].bitcast(F32),
                                      ALU.subtract).then_inc(v_ready, 1)
                    dve.wait_ge(sq_summed, it * 2 + (j + 1))
            HALVES2 = HALVES + N_GROUPS
            dve.wait_ge(ms_half, 1)
            vec.tensor_tensor(sig[:, 0:SEQ], ps[:, 4, 0:SEQ], sig[:, 0:SEQ], ALU.add).then_inc(ms_sum, 1)
            dve.wait_ge(mstd_ready, 1)
            vec.reciprocal(rstd[:, :], sig[:, SEQ:2 * SEQ]).then_inc(mlp_rstd, 1)
            dve.wait_ge(mlp_rstd, 1)

            def chunk(c, last):
                g0 = c * (2 * N_GROUPS) + G_MLP
                h0 = c * (2 * N_GROUPS) + HALVES2
                with dve.Fori(0, N_GROUPS // 2) as it:
                    for j in range(2):
                        g = it * 2 + g0 + j
                        k = c * N_GROUPS + it * 2 + j
                        for u in range(UNITS):
                            split(g + 1, 1 - j, u)
                        sum_half(g, j, it * 2 + h0 + (j + 1))
                        dve.wait_ge(acc_free, g + 1)
                        for t in range(2):
                            last_i = vec.scalar_tensor_tensor(out=relu_b[j][:, t, :], in0=half[:, j, t, :], scalar=0.0,
                                                              in1=rstd[:, :], op0=ALU.max, op1=ALU.mult)
                        last_i.then_inc(relu_ready, 1)
                        dve.wait_ge(hid_hi, k + 1)
                        tiles = bass.ds(it * 4 + 2 * j, 2)
                        vec.tensor_tensor(act_mid[:, tiles, SEQ:2 * SEQ], sq_b[j], act_mid[:, tiles, 0:SEQ].bitcast(F32),
                                          ALU.subtract).then_inc(hid_ready, 1)

                def down(g, j, halves, t0):
                    sum_half(g, j, halves)
                    dve.wait_ge(acc_free, g + 1)
                    tiles = bass.ds(t0, 2)
                    return vec.tensor_tensor(resid[:, tiles, :], resid[:, tiles, :], half[:, j, :, :], ALU.add)

                with dve.Fori(0, N_GROUPS // 2 - last) as it:
                    for j in range(2):
                        g = it * 2 + g0 + (N_GROUPS + j)
                        for u in range(UNITS):
                            split(g + 1, 1 - j, u)
                        down(g, j, it * 2 + h0 + (N_GROUPS + j + 1), it * 4 + 2 * j)
                if last:
                    for u in range(UNITS):
                        split(G_END - 1, 1, u)
                    down(G_END - 2, 0, h0 + 2 * N_GROUPS - 1, KT - 4)
                    down(G_END - 1, 1, h0 + 2 * N_GROUPS, KT - 2).then_inc(dve_done_resid, 1)

            with dve.Fori(0, CHUNKS - 1) as c:
                chunk(c, 0)
            chunk(CHUNKS - 1, 1)

            dve.wait_ge(dve_done_resid, 1)
            for n in range(4):
                dve.wait_ge(fin_sq, n + 1)
                vec.tensor_reduce(sq_acc[:, n % 2, :], stage4[n % 2].rearrange("p t s -> p s t"), AX.X, ALU.add).then_inc(fin_summed, 1)
                dve.wait_ge(fin_summed, n + 1)
                if n == 0:
                    last = vec.tensor_copy(rstd[:, :], sq_acc[:, 0, :])
                else:
                    last = vec.tensor_tensor(rstd[:, :], rstd[:, :], sq_acc[:, n % 2, :], ALU.add)
                last.then_inc(fin_total, 1)
                vec.tensor_tensor(resid[:, 4 * n:4 * n + 4, :], resid[:, 4 * n:4 * n + 4, :],
                                  cols[:, C_FIN + 4 * n:C_FIN + 4 * n + 4].unsqueeze(2).to_broadcast([P, 4, SEQ]),
                                  ALU.mult).then_inc(fin_gained, 1)
                dve.wait_ge(fin_total, n + 1)
            dve.wait_ge(fstd_ready, 1)
            vec.reciprocal(stat[:, 2:4], stat[:, 0:2]).then_inc(frstd_ready, 1)
            dve.wait_ge(frstd_ready, 1)
            for n in range(4):
                dve.wait_ge(y_turned, n + 1)
                vec.tensor_scalar(y_nat[:, D_MODEL + 512 * n:D_MODEL + 512 * n + 512], ps[:, [3, 5, 7, 1][n], :],
                                  stat[:, 3:4], None, ALU.mult).then_inc(y_v, 1)

        @block.tensor
        def _(pe):
            mm = nc.tensor.matmul

            def unit(g, par, u, acts, natural=False, first=False):
                if u == 0 and not first:
                    pe.wait_ge(acc_free, g - 1)
                pe.wait_ge(lo_ready, g * UNITS + (u + 1))
                for t in range(UK):
                    kt = UK * u + t
                    hi, lo = w_hi[:, par * UNITS + u, t, :], w_lo[:, par * UNITS + u, t, :]
                    one, end = kt == 0, kt == KT - 1
                    for b in range(2):
                        part = slice(b * P, b * P + P)
                        if natural:
                            to = ps[:, 2 * par + b, 0:COLS]
                            a_hi, a_lo = acts[:, kt, b * P:b * P + P], acts[:, kt, SEQ + b * P:SEQ + b * P + P]
                            mm(to, a_hi, hi, start=one, stop=False)
                            mm(to, a_hi, lo, start=False, stop=False)
                            last = mm(to, a_lo, hi, start=False, stop=end)
                        else:
                            mm(ps[:, 2 * par + b, :], hi[:, part], acts[:, kt, :], start=one, stop=False)
                            last = mm(ps[:, 2 * par + b, 0:SEQ], lo[:, part], acts[:, kt, 0:SEQ], start=False, stop=end)
                last.then_inc(unit_used, 1)

            pe.wait_ge(const_landed, 16)
            pe.wait_ge(prm_landed, 5 * 16)
            pe.transpose(ps[:, 7, 0:C_ALL], prm[0:C_ALL, :], ident[0:C_ALL, 0:C_ALL]).then_inc(cols_turned, 1)
            pe.wait_ge(x_landed[0], 16)
            pe.wait_ge(x_landed[1], 16)
            for b in range(8):
                if b == 7:
                    pe.wait_ge(cols_ready, 1)
                for t in range(2):
                    for st in range(2):
                        kt = 2 * b + t
                        last = pe.transpose(ps[:, b, t * SEQ + st * P:t * SEQ + st * P + P],
                                            x_nat[st][:, kt * P:kt * P + P], ident[:, :])
                last.then_inc(x_turned, 1)
            pe.wait_ge(diag_ready, 1)
            pe.wait_ge(consts_set, CONSTS)
            pe.wait_ge(resid_v, 1)
            for st in range(2):
                last = mm(ps[:, 0, st * P:st * P + P], ones[:, :], s_x[:, st, :], start=True, stop=True)
            last.then_inc(rstd_spread, 1)

            for u in range(UNITS):
                if u == 0:
                    pe.wait_ge(resid_v, 4)
                    pe.wait_ge(resid_a, 4)
                pe.wait_ge(in_ready, u + 1)
                unit(G_K, 0, u, act_in, first=True)
            for u in range(UNITS):
                unit(G_V, 1, u, act_in, natural=True, first=True)
            with pe.Fori(0, 2) as it:
                for j in range(2):
                    for u in range(UNITS):
                        unit(it * 2 + (G_QA + j), j, u, act_in)

            with pe.Fori(0, ITERS) as it:
                g = it * 4 + G_HG

                def scores():
                    for c in range(2):
                        for n in range(N_CHUNKS):
                            spans = {0: [(0, 0, 64), (64, 0, 64)], 1: [(0, 0, 128)],
                                     2: [(0, 128, 64), (64, 64, 64)], 3: [(0, 128, 128)]}[n]
                            for h in range(2):
                                hs = slice(64 * h, 64 * h + 64)
                                for at, key, w in spans:
                                    last = mm(ps[hs, 4 + c, n * P + at:n * P + at + w],
                                              q_st[hs, c, n * CHUNK:n * CHUNK + CHUNK],
                                              k_st[hs, key:key + w], start=True, stop=True)
                        last.then_inc(scores_ready, 1)

                def turn_probs():
                    for c in range(2):
                        pe.wait_ge(probs_ready, it * 2 + (c + 1))
                        for n in range(N_CHUNKS):
                            last = pe.transpose(ps[:, 6 + c, n * P:n * P + P], probs[c][:, n, :], ident[:, :])
                        last.then_inc(probs_turned, 1)

                def weigh_values():
                    for c in range(2):
                        pe.wait_ge(probs_copied, it * 2 + (c + 1))
                        for n in range(N_CHUNKS):
                            for h in range(2):
                                last = mm(ps[64 * h:64 * h + 64, 4 + c, n * CHUNK:n * CHUNK + CHUNK],
                                          v_st[:, [0, 0, 2, 1][n], :], probs_t[c][:, n, 64 * h:64 * h + 64],
                                          start=True, stop=True)
                    last.then_inc(att_ready, 1)

                def level(i):
                    if i < 8:
                        if i == 0:
                            pe.wait_ge(gates_ready, it * 3 + 2)
                            pe.wait_ge(att_mixed, it + 1)
                        else:
                            pe.wait_ge(level_ready, it * 8 + i)
                        if i >= 2:
                            pe.wait_ge(level_taken, it * 8 + (i - 1))
                        for n in range(4):
                            sl = slice(n * P, n * P + P)
                            a, b = (KK, QS) if i == 0 else (big[:, (i - 1) % 4, :],) * 2
                            last = mm(ps[:, 4 + i % 2, sl], a[:, sl], b[:, sl], start=True, stop=True)
                    else:
                        pe.wait_ge(level_ready, it * 8 + 8)
                        E = big[:, 7 % 4, :]
                        for h in range(2):
                            last = mm(ps[:, 6, h * P:h * P + P], E[:, h * SEQ:h * SEQ + P],
                                      E[:, h * SEQ + P:h * SEQ + SEQ], start=True, stop=True)
                    last.then_inc(level_done, 1)

                def weigh_inputs():
                    pe.wait_ge(level_taken, it * 8 + 8)
                    pe.wait_ge(cross_copied, it + 1)
                    pe.wait_ge(acc_free, g + 3)
                    for h in range(2):
                        hs = slice(h * P, h * P + P)
                        mm(ps[:, 7, h * SEQ:h * SEQ + P], i_nat[:, 0, hs], s_t[:, 2 * h, :], start=True, stop=True)
                        mm(ps[:, 7, h * SEQ + P:h * SEQ + SEQ], i_nat[:, 0, hs], s_x[:, h, :], start=True, stop=False)
                        last = mm(ps[:, 7, h * SEQ + P:h * SEQ + SEQ], i_nat[:, 1, hs], s_t[:, 2 * h + 1, :], start=False, stop=True)
                    last.then_inc(o_ready, 1)

                pe.wait_ge(staged, it + 1)
                unit(g, 0, 0, act_in)
                scores()
                for u in range(1, UNITS):
                    unit(g, 0, u, act_in)

                unit(g + 1, 1, 0, act_in)
                turn_probs()
                unit(g + 1, 1, 1, act_in)
                unit(g + 1, 1, 2, act_in)
                weigh_values()
                unit(g + 1, 1, 3, act_in)

                unit(g + 2, 0, 0, act_in, natural=True)
                unit(g + 2, 0, 1, act_in, natural=True)
                level(0)
                level(1)
                unit(g + 2, 0, 2, act_in, natural=True)
                level(2)
                level(3)
                unit(g + 2, 0, 3, act_in, natural=True)
                level(4)
                level(5)

                unit(g + 3, 1, 0, act_in)
                level(6)
                level(7)
                level(8)
                unit(g + 3, 1, 1, act_in)
                unit(g + 3, 1, 2, act_in)
                weigh_inputs()
                unit(g + 3, 1, 3, act_in)
                pe.wait_ge(osq_ready, it + 1)
                mm(ps[:, 6, :], ones[:, :], big[:, 0, :], start=True, stop=True).then_inc(oms_ready, 1)

            with pe.Fori(0, N_GROUPS // 2) as it:
                for j in range(2):
                    for u in range(UNITS):
                        if u < 2:
                            pe.wait_ge(att_mixed, 2 * u + 2)
                        else:
                            pe.wait_ge(hg_mixed, 2 * u - 2)
                        unit(it * 2 + (G_OUT + j), j, u, act_mid)
            pe.wait_ge(sq_summed, N_GROUPS)
            mm(ps[:, 4, :], ones[:, :], sq_acc.rearrange("p a b -> p (a b)"), start=True, stop=True).then_inc(ms_ready, 1)

            with pe.Fori(0, CHUNKS) as c:
                g0 = c * (2 * N_GROUPS) + G_MLP
                with pe.Fori(0, N_GROUPS // 2) as it:
                    for j in range(2):
                        for u in range(UNITS):
                            pe.wait_ge(v_ready, 2 * u + 2)
                            unit(it * 2 + g0 + j, j, u, act_in)
                with pe.Fori(0, N_GROUPS // 2) as it:
                    for j in range(2):
                        for u in range(UNITS):
                            pe.wait_ge(hid_ready, c * N_GROUPS + (2 * u + 2))
                            unit(it * 2 + g0 + (N_GROUPS + j), j, u, act_mid)

            pe.wait_ge(fin_total, 4)
            for st in range(2):
                last = mm(ps[:, 0, st:st + 1], rstd[:, st * P:st * P + P], ones[:, 0:1], start=True, stop=True)
            last.then_inc(fms_ready, 1)
            for n, b in enumerate((2, 4, 6, 0)):
                pe.wait_ge(fin_gained, n + 1)
                if b == 0:
                    pe.wait_ge(fstd_ready, 1)
                for st in range(2):
                    for t in range(4):
                        last = pe.transpose(ps[:, b + st, t * P:t * P + P],
                                            resid[:, 4 * n + t, st * P:st * P + P], ident[:, :])
                last.then_inc(y_turned, 1)


def kernel(**inputs):
    import numpy as np
    import concourse.bacc as bacc
    from concourse.bass_utils import run_bass_kernel_spmd

    s, t = np.arange(P)[:, None], np.arange(P)[None, :]
    masks = [s == t] + [(s >> n == t >> n) & ((s >> (n - 1)) % 2 == 0) & ((t >> (n - 1)) % 2 == 1) for n in range(1, LEVELS)]
    arrays = {name: np.ascontiguousarray(inputs[name]) for name in (
        "x", "norm_mix", "w_in", "attn_sinks", "lb_logits", "hgrn_norm", "w_out", "norm_mlp",
        "w_up", "w_down", "final_norm")}
    arrays["identity"] = np.eye(P, dtype=np.float32)
    arrays["level_masks"] = np.stack(masks, axis=1).astype(np.float32)

    nc = bacc.Bacc("TRN2", target_bir_lowering=False, num_devices=1)
    args = [nc.dram_tensor(f"in_{name}", a.shape, mybir.dt.from_np(a.dtype), kind="ExternalInput").ap()
            for name, a in arrays.items()]
    out = nc.dram_tensor("out_h", (1, SEQ, D_MODEL), F32, kind="ExternalOutput").ap()
    build(nc, *args, out)
    r = run_bass_kernel_spmd(nc, [{f"in_{name}": a for name, a in arrays.items()}], core_ids=[0])
    return r.results[0]["out_h"]
```

```python
from contextlib import ExitStack

import concourse.bass as bass
from concourse import mybir

F32 = mybir.dt.float32
F32R = mybir.dt.float32r
U8 = mybir.dt.uint8
ACT = mybir.ActivationFunctionType
ALU = mybir.AluOpType
AX = mybir.AxisListType

P = 128
D_MODEL = 2048
SEQ = 256
KT = D_MODEL // P
COLS = 256
UNITS = 4
UK = KT // UNITS
D_FF = 4 * D_MODEL
CHUNKS = D_FF // D_MODEL
N_GROUPS = D_MODEL // COLS
HEAD_DIM = 64
HEADS = 16
KV_HEADS = 4
CHUNK = 64
N_CHUNKS = SEQ // CHUNK
H_HEADS = 8
LEVELS = 8
TAKES = 6
SCALE = HEAD_DIM ** -0.5
EPS = 1e-6

Q_A, K_A, V_A, Q_H, F_H, I_H, G_H = 0, 4, 5, 6, 10, 14, 18
ITERS = 4
G_K, G_V, G_QA, G_HG, G_OUT, G_MLP = 0, 1, 2, 6, 22, 30
G_END = G_MLP + CHUNKS * 2 * N_GROUPS

C_MIX, C_MLP, C_FIN, C_HG, C_LB = 0, 16, 32, 48, 56
C_ALL = 72


def build(nc, x, norm_mix, w_in, attn_sinks, lb_logits, hgrn_norm, w_out, norm_mlp, w_up, w_down,
          final_norm, identity, level_masks, out):
    with ExitStack() as ctx:
        def sb(name, shape, dt=F32):
            return ctx.enter_context(nc.sbuf_tensor(name, shape, dt))

        def sem(name):
            return ctx.enter_context(nc.semaphore(name))

        ps = ctx.enter_context(nc.psum_tensor("ps", [P, 8, 512], F32))

        raw = sb("raw", [P, UNITS, UK, COLS])
        w_hi = sb("w_hi", [P, 2 * UNITS, UK, COLS], F32R)
        w_lo = sb("w_lo", [P, 2 * UNITS, UK, COLS], F32R)
        act_in = sb("act_in", [P, KT, 2 * SEQ], F32R)
        act_mid = sb("act_mid", [P, KT, 2 * SEQ], F32R)
        resid = sb("resid", [P, KT, SEQ])
        qk = sb("qk", [P, 12, SEQ])
        v_all = sb("v_all", [P, 3, COLS])
        q_st = sb("q_st", [P, 2, SEQ])
        k_st = sb("k_st", [P, SEQ])
        v_st = sb("v_st", [P, 3, HEAD_DIM])
        lb_st = sb("lb_st", [P, 2, 2])
        gain_st = sb("gain_st", [P, 2])
        sink_st = sb("sink_st", [P, 2, 2])
        half = sb("half", [P, 2, 2, SEQ])
        big = sb("big", [P, 4, 512])
        hg = sb("hg", [P, 4, 512])
        sig = hg[:, 1, :]
        i_nat = sb("i_nat", [P, 2, COLS])
        s_t = sb("s_t", [P, 4, P])
        s_x = sb("s_x", [P, 2, P])
        ident = sb("ident", [P, P])
        masks = sb("masks", [P, LEVELS, P], U8)
        ones = sb("ones", [P, P])
        cols = sb("cols", [P, C_ALL])
        lbc = sb("lbc", [P, 2, H_HEADS])
        lbe = sb("lbe", [P, 4, H_HEADS])
        sinks_b = sb("sinks_b", [P, HEADS])
        sink_c = sb("sink_c", [P, 2, 8])
        eps_c = sb("eps_c", [P, 1])
        stat = sb("stat", [P, 8])
        wait_mark = sb("wait_mark", [P, LEVELS])
        amax = sb("amax", [P, 2, 4])
        negm = sb("negm", [P, 2, 4])
        asum = sb("asum", [P, 2, 4])
        ssq = sb("ssq", [P, 2, 4])
        esink = sb("esink", [P, 2, 4])
        rstd = sb("rstd", [P, SEQ])

        qa_t = qk[:, 0:8, :]
        k_dup = qk[:, 8:12, :]
        x_nat = [qa_t.rearrange("p a b -> p (a b)"), big[:, :, :].rearrange("p a b -> p (a b)")]
        sq_junk = k_dup.rearrange("p a b -> p (a b)").rearrange("p (a b) -> p a b", a=2)
        mask_f = half[:, :, :, :].rearrange("p a b c -> p (a b c)").rearrange("p (l t) -> p l t", l=LEVELS)
        prm = i_nat[:, 0, 0:P]
        k_t = i_nat
        sq_acc = hg[:, 0, :].rearrange("p (a b) -> p a b", a=2)
        D, U, KK, QS = (hg[:, n, :] for n in range(4))
        probs = [big[:, c, :].rearrange("p (n k) -> p n k", n=4) for c in range(2)]
        probs_t = [big[:, 2 + c, :].rearrange("p (n k) -> p n k", n=4) for c in range(2)]
        U0 = big[:, :, :].rearrange("p a b -> p (a b)")
        stage4 = [U0[:, 1024 * n:1024 * n + 1024].rearrange("p (a b) -> p a b", a=4) for n in range(2)]
        relu_b = [big[:, n, :].rearrange("p (a b) -> p a b", a=2) for n in range(2)]
        sq_b = [big[:, 2 + n, :].rearrange("p (a b) -> p a b", a=2) for n in range(2)]
        y_nat = raw[:, :, :, :].rearrange("p a b c -> p (a b c)").rearrange("p (s n) -> p s n", s=2)
        PIECES = [slice(0, 768), slice(768, 1536)]
        y_tail = [y_nat[:, :, (N_GROUPS - 2 + n) * COLS:(N_GROUPS - 1 + n) * COLS] for n in range(2)]

        raw_landed = [sem(f"raw_landed{n}") for n in range(UNITS)]
        x_landed = [[sem(f"x_landed{st}{n}") for n in range(4)] for st in range(2)]
        prm_landed = sem("prm_landed")
        const_landed = sem("const_landed")
        masks_landed = sem("masks_landed")
        sinks_landed = sem("sinks_landed")
        consts_set = sem("consts_set")
        hi_ready = sem("hi_ready")
        lo_ready = sem("lo_ready")
        unit_used = sem("unit_used")
        half_copied = sem("half_copied")
        acc_free = sem("acc_free")
        dve_step = sem("dve_step")
        act_step = sem("act_step")
        cols_turned = sem("cols_turned")
        cols_ready = sem("cols_ready")
        lb_shifted = sem("lb_shifted")
        lb_exp = sem("lb_exp")
        x_turned = sem("x_turned")
        resid_a = sem("resid_a")
        resid_v = sem("resid_v")
        ssq_a = sem("ssq_a")
        ssq_v = sem("ssq_v")
        ssq_summed = sem("ssq_summed")
        std_ready = sem("std_ready")
        xrstd_ready = sem("xrstd_ready")
        xn_v = sem("xn_v")
        xn_a = sem("xn_a")
        xn_turned = sem("xn_turned")
        in_hi = sem("in_hi")
        in_ready = sem("in_ready")
        kt_ready = sem("kt_ready")
        k_dup_landed = sem("k_dup_landed")
        staged = sem("staged")
        scores_ready = sem("scores_ready")
        negm_ready = sem("negm_ready")
        exp_ready = sem("exp_ready")
        probs_ready = sem("probs_ready")
        probs_turned = sem("probs_turned")
        probs_copied = sem("probs_copied")
        att_ready = sem("att_ready")
        att_hi = sem("att_hi")
        att_mixed = sem("att_mixed")
        sig_ready = sem("sig_ready")
        gates_ready = sem("gates_ready")
        level_ready = sem("level_ready")
        level_done = sem("level_done")
        level_taken = sem("level_taken")
        cross_copied = sem("cross_copied")
        o_ready = sem("o_ready")
        odiag_ready = sem("odiag_ready")
        orstd_spread = sem("orstd_spread")
        osq_ready = sem("osq_ready")
        oms_ready = sem("oms_ready")
        ostd_ready = sem("ostd_ready")
        o_scaled = sem("o_scaled")
        hg_hi = sem("hg_hi")
        hg_mixed = sem("hg_mixed")
        resid_ready = sem("resid_ready")
        scaled_ready = sem("scaled_ready")
        sq_ready = sem("sq_ready")
        v_hi = sem("v_hi")
        v_ready = sem("v_ready")
        sq_summed = sem("sq_summed")
        ms_ready = sem("ms_ready")
        sq_cleared = sem("sq_cleared")
        mstd_ready = sem("mstd_ready")
        relu_ready = sem("relu_ready")
        hid_sq = sem("hid_sq")
        hid_hi = sem("hid_hi")
        hid_ready = sem("hid_ready")
        fin_sq = sem("fin_sq")
        fin_gained = sem("fin_gained")
        resid_done = sem("resid_done")
        y_copied = sem("y_copied")
        fms_ready = sem("fms_ready")
        fstd_ready = sem("fstd_ready")
        frstd_ready = sem("frstd_ready")
        y_turned = sem("y_turned")
        y_a = sem("y_a")
        y_v = sem("y_v")
        y_stored = sem("y_stored")
        mlp_rstd = sem("mlp_rstd")

        block = ctx.enter_context(nc.Block())

        def xn_at(kt):
            return ps[:, 2 + kt // 2 % 6, kt % 2 * SEQ:kt % 2 * SEQ + SEQ]

        def bank_pair(par):
            return ps[:, 2 * par:2 * par + 2, :]

        FIRST_PAIR = [(0, 0), (0, 1)]
        LAST_PAIR = [(3, 0), (3, 1)]

        def is_group(it, j, k):
            return isinstance(it, int) and 2 * it + j == k

        def last_tiles(it, j):
            return slice(4 * it + 2 * j, 4 * it + 2 * j + 2) if isinstance(it, int) else bass.ds(it * 4 + 2 * j, 2)

        def y_slot(it, j):
            return slice(4 * it + 2 * j - 2, 4 * it + 2 * j) if isinstance(it, int) else bass.ds(it * 4 + (2 * j - 2), 2)

        @block.sync
        def _(sp):
            def load(g, par, src, row0, col0, first=False):
                for u in range(UNITS):
                    if not first:
                        sp.wait_ge(lo_ready, g * UNITS + (u - UNITS + 1))
                    rows = row0 + u * UK * P
                    sp.dma_start(
                        raw[:, u, :, :],
                        src[0, bass.ds(rows, UK * P), bass.ds(col0, COLS)].rearrange("(k p) n -> p k n", p=P),
                    ).then_inc(raw_landed[u], 16)

            sp.dma_start(ident[:, :], identity[:, :]).then_inc(const_landed, 16)
            for n in range(4):
                for st in range(2):
                    sp.dma_start(x_nat[st][:, 512 * n:512 * n + 512],
                                 x[0, st * P:(st + 1) * P, 512 * n:512 * n + 512]).then_inc(x_landed[st][n], 16)
            load(G_K, 0, w_in, 0, K_A * COLS, first=True)
            load(G_V, 1, w_in, 0, V_A * COLS)
            with sp.Fori(0, 2) as it:
                for j in range(2):
                    load(it * 2 + (G_QA + j), j, w_in, 0, it * (2 * COLS) + (Q_A + j) * COLS)
            with sp.Fori(0, ITERS) as it:
                for j, part in enumerate((F_H, Q_H, I_H, G_H)):
                    load(it * 4 + (G_HG + j), j % 2, w_in, 0, it * COLS + part * COLS)
            with sp.Fori(0, N_GROUPS // 2) as it:
                for j in range(2):
                    load(it * 2 + (G_OUT + j), j, w_out, 0, it * (2 * COLS) + j * COLS)
            with sp.Fori(0, CHUNKS) as c:
                with sp.Fori(0, N_GROUPS // 2) as it:
                    for j in range(2):
                        load(c * (2 * N_GROUPS) + it * 2 + (G_MLP + j), j, w_up, 0,
                             c * D_MODEL + it * (2 * COLS) + j * COLS)
                with sp.Fori(0, N_GROUPS // 2) as it:
                    for j in range(2):
                        load(c * (2 * N_GROUPS) + it * 2 + (G_MLP + N_GROUPS + j), j, w_down, c * D_MODEL,
                             it * (2 * COLS) + j * COLS)
            for n, piece in enumerate(PIECES):
                for st, ready in ((0, y_v), (1, y_a)):
                    sp.wait_ge(ready, n + 1)
                    sp.dma_start(out[0, st * P:(st + 1) * P, piece], y_nat[:, st, piece]).then_inc(y_stored, 16)
            for n, ready in ((0, y_v), (1, y_a)):
                sp.wait_ge(ready, 3)
                at = (N_GROUPS - 2 + n) * COLS
                sp.dma_start(out[0, :, at:at + COLS].rearrange("(s p) n -> p s n", p=P), y_tail[n]).then_inc(y_stored, 16)
            sp.wait_ge(y_stored, (2 * len(PIECES) + 2) * 16)

        @block.gpsimd
        def _(pool):
            nc.gpsimd.memset(ones[:, :], 1.0).then_inc(consts_set, 1)
            nc.gpsimd.memset(eps_c[:, :], EPS).then_inc(consts_set, 1)
            nc.gpsimd.memset(s_t[:, :, :], 0.0).then_inc(consts_set, 1)

            def stage(it):
                nc.gpsimd.tensor_copy(k_st[:, :], k_dup[:, bass.ds(it, 1), :].rearrange("p a b -> p (a b)"))
                nc.gpsimd.tensor_copy(q_st[:, :, :], qa_t[:, bass.ds(it * 2, 2), :])
                nc.gpsimd.tensor_copy(v_st[:, :, :], v_all[:, :, bass.ds(it * HEAD_DIM, HEAD_DIM)])
                nc.gpsimd.tensor_copy(sink_st[:, :, :], sink_c[:, :, bass.ds(it * 2, 2)]).then_inc(staged, 1)

            pool.wait_ge(k_dup_landed, 64)
            pool.wait_ge(acc_free, G_HG)
            stage(0)
            with pool.Fori(1, ITERS) as it:
                pool.wait_ge(att_ready, it)
                pool.wait_ge(exp_ready, it * 2)
                stage(it)

            pool.wait_ge(sq_summed, N_GROUPS + 1)
            nc.gpsimd.partition_all_reduce(sig[:, 0:SEQ], hg[:, 2, 0:SEQ], P, bass.bass_isa.ReduceOp.add).then_inc(ms_ready, 1)

        CONSTS = 3

        @block.scalar
        def _(act):
            def split(g, par, u, first=False):
                act.wait_ge(raw_landed[u], g * 16 + 16)
                if not first:
                    act.wait_ge(unit_used, g * UNITS + (u + 1 - 2 * UNITS))
                nc.scalar.activation(w_hi[:, par * UNITS + u, :, :], raw[:, u, :, :], ACT.Copy).then_inc(hi_ready, 1)

            def copy_half(g, par):
                act.wait_ge(unit_used, g * UNITS + UNITS)
                nc.scalar.activation(half[:, par, :, :], bank_pair(par)[:, :, SEQ:2 * SEQ], ACT.Copy).then_inc(half_copied, 1)

            for n, (at, src) in enumerate((
                    (C_MIX, norm_mix.rearrange("a (t p) -> (a t) p", p=P)),
                    (C_MLP, norm_mlp.rearrange("a (t p) -> (a t) p", p=P)),
                    (C_FIN, final_norm.rearrange("(t p) -> t p", p=P)),
                    (C_HG, hgrn_norm.rearrange("a (t p) -> (a t) p", p=P)),
                    (C_LB, lb_logits.rearrange("a (t p) -> (a t) p", p=P)))):
                act.dma_start(prm[at:at + src.shape[0], :], src).then_inc(prm_landed, 16)
            act.dma_start(mask_f, level_masks[:, :, :]).then_inc(masks_landed, 16)
            act.dma_start(sinks_b[:, :], attn_sinks[0:1, :].to_broadcast([P, HEADS])).then_inc(sinks_landed, 16)

            act.wait_ge(consts_set, CONSTS)
            nc.scalar.activation(stat[:, 7:8], eps_c[:, 0:1], ACT.Sqrt)
            for n in range(4):
                act.wait_ge(x_landed[0][n], 16)
                nc.scalar.activation(hg[:, n, :], x_nat[0][:, 512 * n:512 * n + 512], ACT.Square,
                                     accum_out=ssq[:, 0, n:n + 1]).then_inc(ssq_a, 1)
                b = 2 * n + 1
                act.wait_ge(x_turned, b + 1)
                nc.scalar.activation(resid[:, 2 * b:2 * b + 2, :], ps[:, b, :].rearrange("p (a b) -> p a b", a=2),
                                     ACT.Copy).then_inc(resid_a, 1)
            act.wait_ge(ssq_summed, 1)
            nc.scalar.activation(stat[:, 2:4], stat[:, 0:2], ACT.Sqrt, bias=eps_c[:, 0:1],
                                 scale=1.0 / D_MODEL).then_inc(std_ready, 1)
            act.wait_ge(xrstd_ready, 1)
            act.wait_ge(x_turned, 8)
            nc.scalar.activation(x_nat[1], x_nat[1], ACT.Copy, scale=stat[:, 5:6]).then_inc(xn_a, 1)
            split(G_K, 0, 0, first=True)
            act.wait_ge(cols_ready, 1)
            for u in range(UNITS):
                act.wait_ge(xn_turned, u + 1)
                for t in range(UK):
                    kt = UK * u + t
                    last = nc.scalar.activation(act_in[:, kt, 0:SEQ], xn_at(kt), ACT.Copy,
                                                scale=cols[:, C_MIX + kt:C_MIX + kt + 1])
                    if t % 2 == 1:
                        last.then_inc(in_hi, 1)
                if u < 3:
                    split(G_K, 0, u + 1, first=True)
            act.wait_ge(lb_shifted, 1)
            nc.scalar.activation(lbe[:, 2:4, :], lbe[:, 0:2, :], ACT.Exp).then_inc(lb_exp, 1)

            for u in range(UNITS):
                split(G_V, 1, u, first=True)
            copy_half(G_K, 0)
            act.wait_ge(kt_ready, 1)
            for to in range(2):
                for frm in range(2):
                    act.dma_start(k_dup[to * 64:to * 64 + 64, frm::2, :], k_t[frm * 64:frm * 64 + 64, :, :]).then_inc(k_dup_landed, 16)
            for u in range(UNITS):
                split(G_QA, 0, u)
            with act.Fori(0, 2) as it:
                for j in range(2):
                    for u in range(UNITS):
                        split(it * 2 + (G_QA + j + 1), 1 - j, u)
                    copy_half(it * 2 + (G_QA + j), j)

            with act.Fori(0, ITERS) as it:
                g = it * 4 + G_HG

                for u in range(UNITS):
                    split(g + 1, 1, u)
                copy_half(g, 0)
                for c in range(2):
                    act.wait_ge(negm_ready, it * 2 + (c + 1))
                    for n in range(N_CHUNKS):
                        w = CHUNK if n == 0 else 2 * CHUNK
                        nc.scalar.activation(probs[c][:, n, 0:w], ps[:, 4 + c, n * P:n * P + w], ACT.Exp,
                                             bias=negm[:, c, n:n + 1], scale=SCALE,
                                             accum_out=asum[:, c, n:n + 1])
                    nc.scalar.activation(esink[:, c, :], negm[:, c, :], ACT.Exp,
                                         bias=sink_st[:, 0, c:c + 1]).then_inc(exp_ready, 1)
                act.wait_ge(acc_free, g + 1)
                nc.scalar.activation(sig[:, :], half[:, 0, :, :].rearrange("p a b -> p (a b)"), ACT.Sigmoid).then_inc(sig_ready, 1)

                for u in range(UNITS):
                    split(g + 2, 0, u)
                    if u == 2:
                        for c in range(2):
                            act.wait_ge(probs_turned, it * 2 + (c + 1))
                            nc.scalar.activation(probs_t[c][0:CHUNK, 0, :], ps[0:CHUNK, 6 + c, 0:P], ACT.Copy)
                            nc.scalar.activation(probs_t[c][:, 1:4, :],
                                                 ps[:, 6 + c, P:4 * P].rearrange("p (n k) -> p n k", n=3),
                                                 ACT.Copy).then_inc(probs_copied, 1)
                copy_half(g + 1, 1)
                act.wait_ge(acc_free, g + 2)
                act.wait_ge(gates_ready, it * 2 + 1)
                nc.scalar.activation(sig[:, :], half[:, 1, :, :].rearrange("p a b -> p (a b)"), ACT.Sigmoid).then_inc(sig_ready, 1)
                act.wait_ge(att_ready, it + 1)
                nc.scalar.activation(act_mid[:, bass.ds(it * 2, 2), 0:SEQ], ps[:, 4:6, 0:SEQ], ACT.Copy).then_inc(att_hi, 1)

                for u in range(UNITS):
                    split(g + 3, 1, u)

                split(g + 4, 0, 0)
                split(g + 4, 0, 1)
                act.wait_ge(level_done, it * 8 + 8)
                nc.scalar.activation(s_x[:, :, :], ps[:, 7, SEQ:2 * SEQ].rearrange("p (h t) -> p h t", h=2), ACT.Copy)
                act.wait_ge(level_taken, it * TAKES + TAKES)
                nc.scalar.activation(s_t[0:64, :, 64:128], ps[0:64, 7, 0:SEQ].rearrange("p (a b) -> p a b", a=4), ACT.Copy)
                for s0 in (0, 64):
                    last = nc.scalar.activation(
                        s_t[s0:s0 + 32, :, s0 + 32:s0 + 64],
                        ps[s0:s0 + 32, 6, :].rearrange("p (a b) -> p a b", a=4)[:, :, s0 + 32:s0 + 64], ACT.Copy)
                last.then_inc(cross_copied, 1)
                split(g + 4, 0, 2)
                act.wait_ge(o_ready, it + 1)
                nc.scalar.activation(big[:, 0, :], ps[:, 7, :], ACT.Square).then_inc(osq_ready, 1)
                nc.scalar.activation(big[:, 2, :], ps[:, 7, :], ACT.Copy)
                act.wait_ge(oms_ready, it + 1)
                nc.scalar.activation(stat[:, 0:4], ps[:, 6, 0:4], ACT.Sqrt, bias=eps_c[:, 0:1], scale=1.0 / P).then_inc(ostd_ready, 1)
                split(g + 4, 0, 3)
                copy_half(g + 3, 1)
                act.wait_ge(acc_free, g + 4)
                nc.scalar.activation(sig[:, :], half[:, 1, :, :].rearrange("p a b -> p (a b)"), ACT.Sigmoid).then_inc(sig_ready, 1)
                act.wait_ge(o_scaled, it + 1)
                nc.scalar.activation(act_mid[:, bass.ds(it * 2 + 8, 2), 0:SEQ],
                                     big[:, 0, :].rearrange("p (h t) -> p h t", h=2), ACT.Copy).then_inc(hg_hi, 1)

            with act.Fori(0, N_GROUPS // 2) as it:
                for j in range(2):
                    g = it * 2 + (G_OUT + j)
                    for u in range(UNITS):
                        split(g + 1, 1 - j, u)
                    copy_half(g, j)
                    act.wait_ge(resid_ready, it * 2 + (j + 1))
                    nc.scalar.activation(sq_b[j], resid[:, bass.ds(it * 4 + 2 * j, 2), :], ACT.Square).then_inc(sq_ready, 1)
                    act.wait_ge(scaled_ready, it * 2 + (j + 1))
                    nc.scalar.activation(act_in[:, bass.ds(it * 4 + 2 * j, 2), 0:SEQ], relu_b[j], ACT.Copy).then_inc(v_hi, 1)
            act.wait_ge(ms_ready, 1)
            nc.scalar.activation(sig[:, SEQ:2 * SEQ], sig[:, 0:SEQ], ACT.Sqrt, bias=eps_c[:, 0:1],
                                 scale=1.0 / D_MODEL).then_inc(mstd_ready, 1)

            def up_step(g, j, n, k):
                for u in range(UNITS):
                    split(g + 1, 1 - j, u)
                copy_half(g, j)
                act.wait_ge(relu_ready, k + 1)
                nc.scalar.activation(sq_b[j], relu_b[j], ACT.Square).then_inc(hid_sq, 1)
                act.wait_ge(hid_sq, k + 1)
                nc.scalar.activation(act_mid[:, bass.ds(n, 2), 0:SEQ], sq_b[j], ACT.Copy).then_inc(hid_hi, 1)

            def chunk(c, last):
                g0 = c * (2 * N_GROUPS) + G_MLP
                with act.Fori(0, N_GROUPS // 2) as it:
                    for j in range(2):
                        up_step(it * 2 + g0 + j, j, it * 4 + 2 * j, c * N_GROUPS + it * 2 + j)
                if not last:
                    with act.Fori(0, N_GROUPS // 2) as it:
                        for j in range(2):
                            g = it * 2 + g0 + (N_GROUPS + j)
                            for u in range(UNITS):
                                split(g + 1, 1 - j, u)
                            copy_half(g, j)

            def last_down(it, j):
                k = it * 2 + j
                g = it * 2 + (G_END - N_GROUPS + j)
                if not is_group(it, j, N_GROUPS - 1):
                    for u in range(UNITS):
                        split(g + 1, 1 - j, u)
                if not (is_group(it, j, 0) or is_group(it, j, N_GROUPS - 1)):
                    act.wait_ge(y_turned, k)
                    nc.scalar.activation(qk[:, y_slot(it, j), :], ps[:, 5 - j, :].rearrange("p (s n) -> p s n", s=2),
                                         ACT.Copy).then_inc(y_copied, 1)
                copy_half(g, j)
                act.wait_ge(resid_done, k + 1)
                nc.scalar.activation(sq_b[j], resid[:, last_tiles(it, j), :], ACT.Square).then_inc(fin_sq, 1)

            with act.Fori(0, CHUNKS - 1) as c:
                chunk(c, 0)
            chunk(CHUNKS - 1, 1)
            for it, j in FIRST_PAIR:
                last_down(it, j)
            with act.Fori(1, N_GROUPS // 2 - 1) as it:
                for j in range(2):
                    last_down(it, j)
            for it, j in LAST_PAIR:
                last_down(it, j)

            act.wait_ge(fms_ready, 1)
            nc.scalar.activation(stat[:, 0:2], ps[:, 6, 0:2], ACT.Sqrt, bias=eps_c[:, 0:1],
                                 scale=1.0 / D_MODEL).then_inc(fstd_ready, 1)
            act.wait_ge(frstd_ready, 1)
            for n in range(2):
                nc.scalar.activation(y_nat[:, 1, PIECES[n]].rearrange("p (k n) -> p k n", k=3),
                                     qk[:, 6 * n + 1:6 * n + 6:2, :], ACT.Copy, scale=stat[:, 3:4]).then_inc(y_a, 1)
            for st in range(2):
                last = nc.scalar.activation(y_tail[1][:, st, :], ps[:, 5, st * SEQ:st * SEQ + SEQ], ACT.Copy,
                                            scale=stat[:, 2 + st:3 + st])
            last.then_inc(y_a, 1)

        @block.vector
        def _(dve):
            vec = nc.vector

            def split(g, par, u):
                dve.wait_ge(hi_ready, g * UNITS + (u + 1))
                s = par * UNITS + u
                vec.tensor_tensor(w_lo[:, s, :, :], raw[:, u, :, :], w_hi[:, s, :, :].bitcast(F32),
                                  ALU.subtract).then_inc(lo_ready, 1)

            def sum_half(g, par, halves, to=None):
                dve.wait_ge(half_copied, halves)
                to = half[:, par, :, :] if to is None else to
                vec.tensor_tensor(to, bank_pair(par)[:, :, 0:SEQ], half[:, par, :, :], ALU.add).then_inc(acc_free, 1)

            steps = [0]

            def link(ins, base=None):
                steps[0] += 1
                ins.then_inc(dve_step, 1)
                dve.wait_ge(dve_step, steps[0] if base is None else base + steps[0])

            for n in range(4):
                dve.wait_ge(x_landed[1][n], 16)
                if n >= 2:
                    dve.wait_ge(ssq_v, n - 1)
                vec.tensor_tensor_reduce(sq_junk[:, n % 2, :], x_nat[1][:, 512 * n:512 * n + 512],
                                         x_nat[1][:, 512 * n:512 * n + 512], 1.0, 0.0, ALU.mult, ALU.add,
                                         ssq[:, 1, n:n + 1]).then_inc(ssq_v, 1)
                b = 2 * n
                dve.wait_ge(x_turned, b + 1)
                vec.tensor_copy(resid[:, 2 * b:2 * b + 2, :],
                                ps[:, b, :].rearrange("p (a b) -> p a b", a=2)).then_inc(resid_v, 1)
            dve.wait_ge(ssq_a, 4)
            dve.wait_ge(ssq_v, 4)
            vec.tensor_reduce(stat[:, 0:2], ssq[:, :, :], AX.X, ALU.add).then_inc(ssq_summed, 1)
            dve.wait_ge(std_ready, 1)
            vec.reciprocal(stat[:, 4:6], stat[:, 2:4]).then_inc(xrstd_ready, 1)
            dve.wait_ge(xrstd_ready, 1)
            dve.wait_ge(x_turned, 8)
            vec.tensor_scalar(x_nat[0], x_nat[0], stat[:, 4:5], None, ALU.mult).then_inc(xn_v, 1)
            dve.wait_ge(cols_turned, 1)
            vec.tensor_copy(cols[:, :], ps[:, 1, 0:C_ALL]).then_inc(cols_ready, 1)
            split(G_K, 0, 0)
            dve.wait_ge(cols_ready, 1)
            for u in range(UNITS):
                for t in range(UK):
                    kt = UK * u + t
                    if t % 2 == 0:
                        dve.wait_ge(in_hi, kt // 2 + 1)
                    last = vec.scalar_tensor_tensor(out=act_in[:, kt, SEQ:2 * SEQ], in0=xn_at(kt),
                                                    scalar=cols[:, C_MIX + kt:C_MIX + kt + 1],
                                                    in1=act_in[:, kt, 0:SEQ].bitcast(F32),
                                                    op0=ALU.mult, op1=ALU.subtract)
                last.then_inc(in_ready, 1)
                if u < 3:
                    split(G_K, 0, u + 1)
            dve.wait_ge(masks_landed, 16)
            vec.tensor_copy(masks[:, :, :], mask_f)
            l0, l1 = cols[:, C_LB:C_LB + 8], cols[:, C_LB + 8:C_LB + 16]
            link(vec.tensor_tensor(lbe[:, 2, :], l0, l1, ALU.max))
            vec.tensor_tensor(lbe[:, 0, :], l0, lbe[:, 2, :], ALU.subtract)
            vec.tensor_tensor(lbe[:, 1, :], l1, lbe[:, 2, :], ALU.subtract).then_inc(lb_shifted, 1)
            dve.wait_ge(lb_exp, 1)
            link(vec.tensor_tensor(lbe[:, 0, :], lbe[:, 2, :], lbe[:, 3, :], ALU.add))
            link(vec.reciprocal(lbe[:, 1, :], lbe[:, 0, :]))
            link(vec.tensor_tensor(lbc[:, 0, :], lbe[:, 2, :], lbe[:, 1, :], ALU.mult))
            link(vec.tensor_scalar(lbc[:, 1, :], lbc[:, 0, :], -1.0, 1.0, ALU.mult, ALU.add))
            dve.wait_ge(sinks_landed, 16)
            for h in range(2):
                vec.tensor_copy(sink_c[64 * h:64 * h + 64, 0, :], sinks_b[64 * h:64 * h + 64, h::2])
                last = vec.tensor_scalar(sink_c[64 * h:64 * h + 64, 1, :], sinks_b[64 * h:64 * h + 64, h::2], -1.0, None, ALU.mult)
            link(last)

            for u in range(UNITS):
                split(G_V, 1, u)
            dve.wait_ge(half_copied, 1)
            vec.tensor_tensor(k_t[:, :, :], bank_pair(0)[:, :, 0:SEQ], half[:, 0, :, :], ALU.add).then_inc(kt_ready, 1)
            dve.wait_ge(kt_ready, 1)
            vec.tensor_copy(stat[:, 6:7], k_t[:, 0, 0:1]).then_inc(acc_free, 1)
            for u in range(UNITS):
                split(G_QA, 0, u)
            dve.wait_ge(unit_used, (G_V + 1) * UNITS)
            vec.tensor_copy(v_all[:, 0:2, :], bank_pair(1)[:, :, 0:COLS])
            vec.tensor_copy(v_all[0:64, 2, :], ps[0:64, 3, 0:COLS])
            vec.tensor_copy(v_all[64:128, 2, :], ps[64:128, 2, 0:COLS]).then_inc(acc_free, 1)
            with dve.Fori(0, 2) as it:
                for j in range(2):
                    for u in range(UNITS):
                        split(it * 2 + (G_QA + j + 1), 1 - j, u)
                    sum_half(it * 2 + (G_QA + j), j, it * 2 + (j + 2), qa_t[:, bass.ds(it * 4 + 2 * j, 2), :])
            dve.wait_ge(acc_free, G_HG)

            def levels_view(t, n):
                return t.rearrange("p (b two n) -> p b two n", two=2, n=n)

            PER_ITER = 24
            pre = steps[0]
            with dve.Fori(0, ITERS) as it:
                steps[0] = pre
                base = it * PER_ITER
                g = it * 4 + G_HG
                lv = it * 8
                n_e = it * 8

                vec.tensor_copy(lb_st[:, :, :], lbc[:, :, bass.ds(it * 2, 2)])
                vec.tensor_copy(gain_st[:, :], cols[:, bass.ds(it * 2 + C_HG, 2)])
                for u in range(UNITS):
                    split(g + 1, 1, u)
                dve.wait_ge(staged, it + 1)
                for c in range(2):
                    dve.wait_ge(scores_ready, it * 2 + (c + 1))
                    link(vec.tensor_reduce(amax[:, c, :], ps[:, 4 + c, :].rearrange("p (n k) -> p n k", n=4),
                                           AX.X, ALU.max), base)
                    vec.tensor_scalar(negm[:, c, :], amax[:, c, :], -SCALE, sink_st[:, 1, c:c + 1],
                                      ALU.mult, ALU.min).then_inc(negm_ready, 1)
                sum_half(g, 0, it * 3 + 6)
                for c in range(2):
                    dve.wait_ge(exp_ready, it * 2 + (c + 1))
                    link(vec.tensor_tensor(asum[:, c, :], asum[:, c, :], esink[:, c, :], ALU.add), base)
                    link(vec.reciprocal(esink[:, c, :], asum[:, c, :]), base)
                    vec.tensor_scalar(probs[c][:, 0, 0:CHUNK], probs[c][:, 0, 0:CHUNK], esink[:, c, 0:1], None, ALU.mult)
                    vec.tensor_tensor(probs[c][:, 1:4, :], probs[c][:, 1:4, :],
                                      esink[:, c, 1:4].unsqueeze(2).to_broadcast([P, 3, P]), ALU.mult).then_inc(probs_ready, 1)
                dve.wait_ge(sig_ready, it * 3 + 1)
                for h in range(2):
                    sl = slice(h * SEQ, h * SEQ + SEQ)
                    last = vec.tensor_scalar(D[:, sl], sig[:, sl], lb_st[:, 1, h:h + 1], lb_st[:, 0, h:h + 1], ALU.mult, ALU.add)
                last.then_inc(gates_ready, 1)
                dve.wait_ge(gates_ready, it * 2 + 1)
                link(vec.tensor_scalar(KK, D, -1.0, 1.0, ALU.mult, ALU.add), base)

                for u in range(UNITS):
                    split(g + 2, 0, u)
                sum_half(g + 1, 1, it * 3 + 7)
                dve.wait_ge(sig_ready, it * 3 + 2)
                dve.wait_ge(acc_free, g + 2)
                vec.tensor_tensor(QS, half[:, 1, :, :].rearrange("p a b -> p (a b)"), sig[:, :], ALU.mult).then_inc(gates_ready, 1)
                dve.wait_ge(gates_ready, it * 2 + 2)

                def settle():
                    dve.wait_ge(dve_step, base + steps[0])

                def mark(ins):
                    steps[0] += 1
                    ins.then_inc(dve_step, 1)

                def operand(l):
                    n = 1 << l
                    E = levels_view(big[:, l % 4, :], n)
                    d, uu, kk, qq = (levels_view(t, n) for t in (D, U, KK, QS))
                    if l:
                        settle()
                    if l >= 4:
                        dve.wait_ge(level_done, lv + (l - 4 + 2))
                    if l == 0:
                        vec.tensor_copy(E[:, :, 0, :], kk[:, :, 0, :])
                    else:
                        vec.tensor_tensor(E[:, :, 0, :], kk[:, :, 0, :], uu[:, :, 0, :], ALU.mult)
                    vec.tensor_tensor(E[:, :, 1, :], qq[:, :, 1, :], d[:, :, 1, :], ALU.mult).then_inc(level_ready, 1)

                def extend_u(l):
                    n = 1 << l
                    d, uu = levels_view(D, n), levels_view(U, n)
                    if l == 0:
                        vec.memset(uu[:, :, 1, :], 1.0)
                        mark(vec.tensor_copy(uu[:, :, 0, :], d[:, :, 1, :]))
                    else:
                        mark(vec.tensor_tensor(uu[:, :, 0, :], uu[:, :, 0, :],
                                               d[:, :, 1, n - 1:n].to_broadcast([P, 512 // (2 * n), n]), ALU.mult))

                def extend_d(l):
                    n = 1 << l
                    d = levels_view(D, n)
                    settle()
                    mark(vec.tensor_tensor(d[:, :, 1, :], d[:, :, 1, :],
                                           d[:, :, 0, n - 1:n].to_broadcast([P, 512 // (2 * n), n]), ALU.mult))

                def take(i):
                    dve.wait_ge(level_done, lv + (i + 1))
                    if i:
                        dve.wait_ge(level_taken, it * TAKES + i)
                    vec.memset(wait_mark[:, i:i + 1], 0.0)
                    vec.copy_predicated(s_t[:, :, :], masks[:, i:i + 1, :].to_broadcast([P, 4, P]),
                                        ps[:, 4 + i % 4, :].rearrange("p (a b) -> p a b", a=4)).then_inc(level_taken, 1)

                operand(0)
                extend_u(0)
                dve.wait_ge(att_hi, it + 1)
                at = act_mid[:, bass.ds(it * 2, 2), :]
                vec.tensor_tensor(at[:, :, SEQ:2 * SEQ], ps[:, 4:6, 0:SEQ], at[:, :, 0:SEQ].bitcast(F32),
                                  ALU.subtract).then_inc(att_mixed, 1)
                extend_d(0)
                operand(1)
                extend_u(1)
                split(g + 3, 1, 0)
                extend_d(1)
                operand(2)
                extend_u(2)
                split(g + 3, 1, 1)
                extend_d(2)
                operand(3)
                extend_u(3)
                take(0)
                extend_d(3)
                take(1)
                operand(4)
                extend_u(4)
                take(2)
                extend_d(4)
                operand(5)
                extend_u(5)
                take(3)
                extend_d(5)
                operand(6)
                extend_u(6)
                split(g + 3, 1, 2)
                extend_d(6)
                operand(7)
                take(4)
                dve.wait_ge(unit_used, g * UNITS + 3 * UNITS)
                vec.tensor_copy(i_nat[:, :, :], bank_pair(0)[:, :, 0:COLS]).then_inc(acc_free, 1)
                take(5)
                split(g + 3, 1, 3)

                split(g + 4, 0, 0)
                split(g + 4, 0, 1)
                split(g + 4, 0, 2)
                dve.wait_ge(ostd_ready, it + 1)
                link(vec.reciprocal(stat[:, 4:8], stat[:, 0:4]), base)
                vec.tensor_tensor(big[:, 1, :].rearrange("p (n t) -> p n t", n=4),
                                  ident[:, :].unsqueeze(1).to_broadcast([P, 4, P]),
                                  stat[:, 4:8].unsqueeze(2).to_broadcast([P, 4, P]), ALU.mult).then_inc(odiag_ready, 1)
                split(g + 4, 0, 3)
                dve.wait_ge(orstd_spread, it + 1)
                for h in range(2):
                    sl = slice(h * SEQ, h * SEQ + SEQ)
                    last = vec.scalar_tensor_tensor(out=big[:, 3, sl], in0=ps[:, 6, sl], scalar=gain_st[:, h:h + 1],
                                                    in1=big[:, 2, sl], op0=ALU.mult, op1=ALU.mult)
                link(last, base)
                sum_half(g + 3, 1, it * 3 + 8)
                dve.wait_ge(acc_free, g + 4)
                link(vec.tensor_tensor(big[:, 3, :], half[:, 1, :, :].rearrange("p a b -> p (a b)"), big[:, 3, :], ALU.mult), base)
                dve.wait_ge(sig_ready, it * 3 + 3)
                vec.tensor_tensor(big[:, 0, :], big[:, 3, :], sig[:, :], ALU.mult).then_inc(o_scaled, 1)
                dve.wait_ge(hg_hi, it + 1)
                at = act_mid[:, bass.ds(it * 2 + 8, 2), :]
                vec.tensor_tensor(at[:, :, SEQ:2 * SEQ], big[:, 0, :].rearrange("p (h t) -> p h t", h=2),
                                  at[:, :, 0:SEQ].bitcast(F32), ALU.subtract).then_inc(hg_mixed, 1)
                PER = steps[0] - pre
            assert PER == PER_ITER, PER
            HALVES = 1 + 4 + 3 * ITERS
            after = PER_ITER * ITERS - PER_ITER

            link(vec.memset(sq_acc, 0.0), after)
            with dve.Fori(0, N_GROUPS // 2) as it:
                for j in range(2):
                    g = it * 2 + (G_OUT + j)
                    for u in range(UNITS):
                        split(g + 1, 1 - j, u)
                    sum_half(g, j, it * 2 + (HALVES + j + 1))
                    dve.wait_ge(acc_free, g + 1)
                    tiles = bass.ds(it * 4 + 2 * j, 2)
                    vec.tensor_tensor(resid[:, tiles, :], resid[:, tiles, :], half[:, j, :, :], ALU.add).then_inc(resid_ready, 1)
                    dve.wait_ge(resid_ready, it * 2 + (j + 1))
                    vec.tensor_tensor(relu_b[j], resid[:, tiles, :],
                                      cols[:, bass.ds(it * 4 + (C_MLP + 2 * j), 2)].unsqueeze(2).to_broadcast([P, 2, SEQ]),
                                      ALU.mult).then_inc(scaled_ready, 1)
                    dve.wait_ge(sq_ready, it * 2 + (j + 1))
                    vec.tensor_tensor(sq_acc, sq_acc, sq_b[j], ALU.add).then_inc(sq_summed, 1)
                    dve.wait_ge(v_hi, it * 2 + (j + 1))
                    vec.tensor_tensor(act_in[:, tiles, SEQ:2 * SEQ], relu_b[j], act_in[:, tiles, 0:SEQ].bitcast(F32),
                                      ALU.subtract).then_inc(v_ready, 1)
                    dve.wait_ge(sq_summed, it * 2 + (j + 1))
            HALVES2 = HALVES + N_GROUPS
            vec.tensor_tensor(hg[:, 2, 0:SEQ], sq_acc[:, 0, :], sq_acc[:, 1, :], ALU.add).then_inc(sq_summed, 1)
            dve.wait_ge(sq_summed, N_GROUPS + 1)
            vec.memset(sq_acc, 0.0).then_inc(sq_cleared, 1)
            dve.wait_ge(mstd_ready, 1)
            vec.reciprocal(rstd[:, :], sig[:, SEQ:2 * SEQ]).then_inc(mlp_rstd, 1)
            dve.wait_ge(mlp_rstd, 1)

            def chunk(c, last):
                g0 = c * (2 * N_GROUPS) + G_MLP
                h0 = c * (2 * N_GROUPS) + HALVES2
                with dve.Fori(0, N_GROUPS // 2) as it:
                    for j in range(2):
                        g = it * 2 + g0 + j
                        k = c * N_GROUPS + it * 2 + j
                        for u in range(UNITS):
                            split(g + 1, 1 - j, u)
                        sum_half(g, j, it * 2 + h0 + (j + 1))
                        dve.wait_ge(acc_free, g + 1)
                        for t in range(2):
                            last_i = vec.scalar_tensor_tensor(out=relu_b[j][:, t, :], in0=half[:, j, t, :], scalar=0.0,
                                                              in1=rstd[:, :], op0=ALU.max, op1=ALU.mult)
                        last_i.then_inc(relu_ready, 1)
                        dve.wait_ge(hid_hi, k + 1)
                        tiles = bass.ds(it * 4 + 2 * j, 2)
                        vec.tensor_tensor(act_mid[:, tiles, SEQ:2 * SEQ], sq_b[j], act_mid[:, tiles, 0:SEQ].bitcast(F32),
                                          ALU.subtract).then_inc(hid_ready, 1)

                if not last:
                    with dve.Fori(0, N_GROUPS // 2) as it:
                        for j in range(2):
                            g = it * 2 + g0 + (N_GROUPS + j)
                            for u in range(UNITS):
                                split(g + 1, 1 - j, u)
                            sum_half(g, j, it * 2 + h0 + (N_GROUPS + j + 1))
                            dve.wait_ge(acc_free, g + 1)
                            tiles = bass.ds(it * 4 + 2 * j, 2)
                            vec.tensor_tensor(resid[:, tiles, :], resid[:, tiles, :], half[:, j, :, :], ALU.add)

            def last_down(it, j):
                k = it * 2 + j
                g = it * 2 + (G_END - N_GROUPS + j)
                if not is_group(it, j, N_GROUPS - 1):
                    for u in range(UNITS):
                        split(g + 1, 1 - j, u)
                sum_half(g, j, it * 2 + (HALVES2 + CHUNKS * 2 * N_GROUPS - N_GROUPS + j + 1))
                dve.wait_ge(acc_free, g + 1)
                tiles = last_tiles(it, j)
                vec.tensor_tensor(resid[:, tiles, :], resid[:, tiles, :], half[:, j, :, :], ALU.add).then_inc(resid_done, 1)
                dve.wait_ge(resid_done, k + 1)
                if not (is_group(it, j, 0) or is_group(it, j, 1)):
                    dve.wait_ge(y_turned, k - 1)
                gains = slice(C_FIN + 4 * it + 2 * j, C_FIN + 4 * it + 2 * j + 2) if isinstance(it, int) \
                    else bass.ds(it * 4 + (C_FIN + 2 * j), 2)
                vec.tensor_tensor(relu_b[j], resid[:, tiles, :], cols[:, gains].unsqueeze(2).to_broadcast([P, 2, SEQ]),
                                  ALU.mult).then_inc(fin_gained, 1)
                dve.wait_ge(fin_sq, k + 1)
                dve.wait_ge(sq_cleared, k + 1)
                vec.tensor_tensor(sq_acc, sq_acc, sq_b[j], ALU.add).then_inc(sq_cleared, 1)

            with dve.Fori(0, CHUNKS - 1) as c:
                chunk(c, 0)
            chunk(CHUNKS - 1, 1)
            for it, j in FIRST_PAIR:
                last_down(it, j)
            with dve.Fori(1, N_GROUPS // 2 - 1) as it:
                for j in range(2):
                    last_down(it, j)
            for it, j in LAST_PAIR:
                last_down(it, j)

            dve.wait_ge(fstd_ready, 1)
            vec.reciprocal(stat[:, 2:4], stat[:, 0:2]).then_inc(frstd_ready, 1)
            dve.wait_ge(frstd_ready, 1)
            dve.wait_ge(y_copied, N_GROUPS - 2)
            for n in range(2):
                vec.tensor_scalar(y_nat[:, 0, PIECES[n]].rearrange("p (k n) -> p k n", k=3),
                                  qk[:, 6 * n:6 * n + 6:2, :], stat[:, 2:3], None, ALU.mult).then_inc(y_v, 1)
            for st in range(2):
                last = vec.tensor_scalar(y_tail[0][:, st, :], ps[:, 4, st * SEQ:st * SEQ + SEQ], stat[:, 2 + st:3 + st],
                                         None, ALU.mult)
            last.then_inc(y_v, 1)

        @block.tensor
        def _(pe):
            mm = nc.tensor.matmul

            def unit(g, par, u, acts, natural=False, first=False):
                if u == 0 and not first:
                    pe.wait_ge(acc_free, g - 1)
                pe.wait_ge(lo_ready, g * UNITS + (u + 1))
                for t in range(UK):
                    kt = UK * u + t
                    hi, lo = w_hi[:, par * UNITS + u, t, :], w_lo[:, par * UNITS + u, t, :]
                    one, end = kt == 0, kt == KT - 1
                    for b in range(2):
                        part = slice(b * P, b * P + P)
                        if natural:
                            to = ps[:, 2 * par + b, 0:COLS]
                            a_hi, a_lo = acts[:, kt, b * P:b * P + P], acts[:, kt, SEQ + b * P:SEQ + b * P + P]
                            mm(to, a_hi, hi, start=one, stop=False)
                            mm(to, a_hi, lo, start=False, stop=False)
                            last = mm(to, a_lo, hi, start=False, stop=end)
                        else:
                            mm(ps[:, 2 * par + b, :], hi[:, part], acts[:, kt, :], start=one, stop=False)
                            last = mm(ps[:, 2 * par + b, 0:SEQ], lo[:, part], acts[:, kt, 0:SEQ], start=False, stop=end)
                last.then_inc(unit_used, 1)

            pe.wait_ge(const_landed, 16)
            for b in range(8):
                if b % 2 == 0:
                    pe.wait_ge(x_landed[0][b // 2], 16)
                    pe.wait_ge(x_landed[1][b // 2], 16)
                for t in range(2):
                    for st in range(2):
                        kt = 2 * b + t
                        last = pe.transpose(ps[:, b, t * SEQ + st * P:t * SEQ + st * P + P],
                                            x_nat[st][:, kt * P:kt * P + P], ident[:, :])
                last.then_inc(x_turned, 1)
            pe.wait_ge(prm_landed, 5 * 16)
            pe.wait_ge(resid_a, 1)
            pe.transpose(ps[:, 1, 0:C_ALL], prm[0:C_ALL, :], ident[0:C_ALL, 0:C_ALL]).then_inc(cols_turned, 1)

            def turn_xn(u):
                for kt in range(UK * u, UK * u + UK):
                    for st in range(2):
                        last = pe.transpose(xn_at(kt)[:, st * P:st * P + P], x_nat[st][:, kt * P:kt * P + P], ident[:, :])
                last.then_inc(xn_turned, 1)

            pe.wait_ge(xn_v, 1)
            pe.wait_ge(xn_a, 1)
            pe.wait_ge(resid_v, 4)
            pe.wait_ge(resid_a, 4)
            for u in range(3):
                turn_xn(u)
            pe.wait_ge(in_ready, 1)
            unit(G_K, 0, 0, act_in, first=True)
            turn_xn(3)
            for u in range(1, UNITS):
                pe.wait_ge(in_ready, u + 1)
                unit(G_K, 0, u, act_in, first=True)
            for u in range(UNITS):
                unit(G_V, 1, u, act_in, natural=True, first=True)
            with pe.Fori(0, 2) as it:
                for j in range(2):
                    for u in range(UNITS):
                        unit(it * 2 + (G_QA + j), j, u, act_in)

            with pe.Fori(0, ITERS) as it:
                g = it * 4 + G_HG

                def scores():
                    for c in range(2):
                        for n in range(N_CHUNKS):
                            spans = {0: [(0, 0, 64), (64, 0, 64)], 1: [(0, 0, 128)],
                                     2: [(0, 128, 64), (64, 64, 64)], 3: [(0, 128, 128)]}[n]
                            for h in range(2):
                                hs = slice(64 * h, 64 * h + 64)
                                for at, key, w in spans:
                                    last = mm(ps[hs, 4 + c, n * P + at:n * P + at + w],
                                              q_st[hs, c, n * CHUNK:n * CHUNK + CHUNK],
                                              k_st[hs, key:key + w], start=True, stop=True)
                        last.then_inc(scores_ready, 1)

                def turn_probs():
                    for c in range(2):
                        pe.wait_ge(probs_ready, it * 2 + (c + 1))
                        for n in (1, 2, 3, 0):
                            w = CHUNK if n == 0 else 2 * CHUNK
                            last = pe.transpose(ps[0:w, 6 + c, n * P:n * P + P], probs[c][:, n, 0:w], ident[:, :])
                        last.then_inc(probs_turned, 1)

                def weigh_values():
                    for c in range(2):
                        pe.wait_ge(probs_copied, it * 2 + (c + 1))
                        for n in (1, 2, 3, 0):
                            for h in range(2):
                                w = CHUNK if n == 0 else 2 * CHUNK
                                last = mm(ps[64 * h:64 * h + 64, 4 + c, n * CHUNK:n * CHUNK + CHUNK],
                                          v_st[0:w, [0, 0, 2, 1][n], :], probs_t[c][0:w, n, 64 * h:64 * h + 64],
                                          start=True, stop=True)
                    last.then_inc(att_ready, 1)

                def level(i):
                    if i == 0:
                        pe.wait_ge(gates_ready, it * 2 + 2)
                        pe.wait_ge(att_mixed, it + 1)
                    else:
                        pe.wait_ge(level_ready, it * 8 + i)
                    if i >= 4:
                        pe.wait_ge(level_taken, it * TAKES + (i - 3))
                    for n in range(4):
                        sl = slice(n * P, n * P + P)
                        a, b = (KK, QS) if i == 0 else (big[:, (i - 1) % 4, :],) * 2
                        last = mm(ps[:, 4 + i % 4, sl], a[:, sl], b[:, sl], start=True, stop=True)
                    last.then_inc(level_done, 1)

                def wide_levels():
                    pe.wait_ge(level_ready, it * 8 + 8)
                    pe.wait_ge(level_taken, it * TAKES + 4)
                    E = big[:, 7 % 4, :]
                    for h in range(2):
                        mm(ps[:, 7, SEQ + h * P:SEQ + h * P + P], E[:, h * SEQ:h * SEQ + P],
                           E[:, h * SEQ + P:h * SEQ + SEQ], start=True, stop=True)
                    E = big[:, 6 % 4, :]
                    for n in range(4):
                        last = mm(ps[0:64, 7, n * 64:n * 64 + 64], E[:, n * P:n * P + 64],
                                  E[:, n * P + 64:n * P + P], start=True, stop=True)
                    last.then_inc(level_done, 1)

                def weigh_inputs():
                    pe.wait_ge(cross_copied, it + 1)
                    pe.wait_ge(acc_free, g + 3)
                    for h in range(2):
                        hs = slice(h * P, h * P + P)
                        mm(ps[:, 7, h * SEQ:h * SEQ + P], i_nat[:, 0, hs], s_t[:, 2 * h, :], start=True, stop=True)
                        mm(ps[:, 7, h * SEQ + P:h * SEQ + SEQ], i_nat[:, 0, hs], s_x[:, h, :], start=True, stop=False)
                        last = mm(ps[:, 7, h * SEQ + P:h * SEQ + SEQ], i_nat[:, 1, hs], s_t[:, 2 * h + 1, :], start=False, stop=True)
                    last.then_inc(o_ready, 1)

                unit(g, 0, 0, act_in)
                unit(g, 0, 1, act_in)
                pe.wait_ge(staged, it + 1)
                unit(g, 0, 2, act_in)
                scores()
                unit(g, 0, 3, act_in)

                unit(g + 1, 1, 0, act_in)
                unit(g + 1, 1, 1, act_in)
                turn_probs()
                unit(g + 1, 1, 2, act_in)
                unit(g + 1, 1, 3, act_in)
                weigh_values()

                unit(g + 2, 0, 0, act_in, natural=True)
                unit(g + 2, 0, 1, act_in, natural=True)
                level(0)
                level(1)
                unit(g + 2, 0, 2, act_in, natural=True)
                level(2)
                level(3)
                unit(g + 2, 0, 3, act_in, natural=True)
                level(4)
                level(5)

                unit(g + 3, 1, 0, act_in)
                level(6)
                wide_levels()
                unit(g + 3, 1, 1, act_in)
                weigh_inputs()
                unit(g + 3, 1, 2, act_in)
                pe.wait_ge(osq_ready, it + 1)
                for n in range(4):
                    last = mm(ps[:, 6, n:n + 1], big[:, 0, n * P:n * P + P], ones[:, 0:1], start=True, stop=True)
                last.then_inc(oms_ready, 1)
                unit(g + 3, 1, 3, act_in)
                pe.wait_ge(odiag_ready, it + 1)
                mm(ps[:, 6, :], ones[:, :], big[:, 1, :], start=True, stop=True).then_inc(orstd_spread, 1)

            with pe.Fori(0, N_GROUPS // 2) as it:
                for j in range(2):
                    for u in range(UNITS):
                        if u < 2:
                            pe.wait_ge(att_mixed, 2 * u + 2)
                        else:
                            pe.wait_ge(hg_mixed, 2 * u - 2)
                        unit(it * 2 + (G_OUT + j), j, u, act_mid)
            def up(g0):
                with pe.Fori(0, N_GROUPS // 2) as it:
                    for j in range(2):
                        for u in range(UNITS):
                            pe.wait_ge(v_ready, 2 * u + 2)
                            unit(it * 2 + g0 + j, j, u, act_in)

            with pe.Fori(0, CHUNKS - 1) as c:
                g0 = c * (2 * N_GROUPS) + G_MLP
                up(g0)
                with pe.Fori(0, N_GROUPS // 2) as it:
                    for j in range(2):
                        for u in range(UNITS):
                            pe.wait_ge(hid_ready, c * N_GROUPS + (2 * u + 2))
                            unit(it * 2 + g0 + (N_GROUPS + j), j, u, act_mid)
            up(G_END - 2 * N_GROUPS)

            def turn_y(b, ready):
                pe.wait_ge(fin_gained, ready)
                for st in range(2):
                    for t in range(2):
                        last = pe.transpose(ps[:, b, st * SEQ + t * P:st * SEQ + t * P + P],
                                            relu_b[b - 4][:, t, st * P:st * P + P], ident[:, :])
                last.then_inc(y_turned, 1)

            def last_down(it, j):
                for u in range(UNITS):
                    pe.wait_ge(hid_ready, (CHUNKS - 1) * N_GROUPS + 2 * u + 2)
                    unit(it * 2 + (G_END - N_GROUPS + j), j, u, act_mid)
                    if u == 2 and not is_group(it, j, 0):
                        turn_y(5 - j, it * 2 + j)

            for it, j in FIRST_PAIR:
                last_down(it, j)
            with pe.Fori(1, N_GROUPS // 2 - 1) as it:
                for j in range(2):
                    last_down(it, j)
            for it, j in LAST_PAIR:
                last_down(it, j)
            turn_y(5, N_GROUPS)
            pe.wait_ge(sq_cleared, N_GROUPS + 1)
            for st in range(2):
                for a in range(2):
                    last = mm(ps[:, 6, st:st + 1], sq_acc[:, a, st * P:st * P + P], ones[:, 0:1], start=a == 0, stop=a == 1)
            last.then_inc(fms_ready, 1)


def kernel(**inputs):
    import numpy as np
    import concourse.bacc as bacc
    from concourse.bass_utils import run_bass_kernel_spmd

    s, t = np.arange(P)[:, None], np.arange(P)[None, :]
    masks = [s == t] + [(s >> n == t >> n) & ((s >> (n - 1)) % 2 == 0) & ((t >> (n - 1)) % 2 == 1) for n in range(1, LEVELS)]
    arrays = {name: np.ascontiguousarray(inputs[name]) for name in (
        "x", "norm_mix", "w_in", "attn_sinks", "lb_logits", "hgrn_norm", "w_out", "norm_mlp",
        "w_up", "w_down", "final_norm")}
    arrays["identity"] = np.eye(P, dtype=np.float32)
    arrays["level_masks"] = np.stack(masks, axis=1).astype(np.float32)

    nc = bacc.Bacc("TRN2", target_bir_lowering=False, num_devices=1)
    args = [nc.dram_tensor(f"in_{name}", a.shape, mybir.dt.from_np(a.dtype), kind="ExternalInput").ap()
            for name, a in arrays.items()]
    out = nc.dram_tensor("out_h", (1, SEQ, D_MODEL), F32, kind="ExternalOutput").ap()
    build(nc, *args, out)
    r = run_bass_kernel_spmd(nc, [{f"in_{name}": a for name, a in arrays.items()}], core_ids=[0])
    return r.results[0]["out_h"]
```

```python
from contextlib import ExitStack

import concourse.bass as bass
from concourse import mybir

F32 = mybir.dt.float32
F32R = mybir.dt.float32r
U8 = mybir.dt.uint8
ACT = mybir.ActivationFunctionType
ALU = mybir.AluOpType
AX = mybir.AxisListType

P = 128
D_MODEL = 2048
SEQ = 256
KT = D_MODEL // P
COLS = 256
UNITS = 4
UK = KT // UNITS
D_FF = 4 * D_MODEL
CHUNKS = D_FF // D_MODEL
N_GROUPS = D_MODEL // COLS
HEAD_DIM = 64
HEADS = 16
KV_HEADS = 4
CHUNK = 64
N_CHUNKS = SEQ // CHUNK
H_HEADS = 8
LEVELS = 8
TAKES = 6
SCALE = HEAD_DIM ** -0.5
EPS = 1e-6

Q_A, K_A, V_A, Q_H, F_H, I_H, G_H = 0, 4, 5, 6, 10, 14, 18
ITERS = 4
G_K, G_V, G_QA, G_HG, G_OUT, G_MLP = 0, 1, 2, 6, 22, 30
G_END = G_MLP + CHUNKS * 2 * N_GROUPS

C_MLP, C_FIN, C_HG, C_LB, C_MIX = 0, 16, 32, 40, 56
C_ALL = 72


def build(nc, x, norm_mix, w_in, attn_sinks, lb_logits, hgrn_norm, w_out, norm_mlp, w_up, w_down,
          final_norm, identity, level_masks, out):
    with ExitStack() as ctx:
        def sb(name, shape, dt=F32):
            return ctx.enter_context(nc.sbuf_tensor(name, shape, dt))

        def sem(name):
            return ctx.enter_context(nc.semaphore(name))

        ps = ctx.enter_context(nc.psum_tensor("ps", [P, 8, 512], F32))

        raw = sb("raw", [P, UNITS, UK, COLS])
        w_hi = sb("w_hi", [P, 2 * UNITS, UK, COLS], F32R)
        w_lo = sb("w_lo", [P, 2 * UNITS, UK, COLS], F32R)
        act_in = sb("act_in", [P, KT, 2 * SEQ], F32R)
        act_mid = sb("act_mid", [P, KT, 2 * SEQ], F32R)
        resid = sb("resid", [P, KT, SEQ])
        qk = sb("qk", [P, 12, SEQ])
        v_all = sb("v_all", [P, 3, COLS])
        q_st = sb("q_st", [P, 2, SEQ])
        k_st = sb("k_st", [P, SEQ])
        v_st = sb("v_st", [P, 3, HEAD_DIM])
        lb_st = sb("lb_st", [P, 2, 2])
        gain_st = sb("gain_st", [P, 2])
        sink_st = sb("sink_st", [P, 2, 2])
        half = sb("half", [P, 2, 2, SEQ])
        big = sb("big", [P, 4, 512])
        hg = sb("hg", [P, 4, 512])
        sig = hg[:, 1, :]
        i_nat = sb("i_nat", [P, 2, COLS])
        s_t = sb("s_t", [P, 4, P])
        s_x = sb("s_x", [P, 2, P])
        ident = sb("ident", [P, P])
        masks = sb("masks", [P, TAKES, P], U8)
        ones = sb("ones", [P, P])
        cols = sb("cols", [P, C_ALL])
        lbc = sb("lbc", [P, 2, H_HEADS])
        lbe = sb("lbe", [P, 4, H_HEADS])
        sinks_b = sb("sinks_b", [P, HEADS])
        sink_c = sb("sink_c", [P, 2, 8])
        eps_c = sb("eps_c", [P, 1])
        stat = sb("stat", [P, 8])
        wait_mark = sb("wait_mark", [P, TAKES])
        amax = sb("amax", [P, 2, 4])
        negm = sb("negm", [P, 2, 4])
        asum = sb("asum", [P, 2, 4])
        ssq = sb("ssq", [P, 2, 4])
        esink = sb("esink", [P, 2, 4])
        rstd = sb("rstd", [P, SEQ])

        qa_t = qk[:, 0:8, :]
        k_dup = qk[:, 8:12, :]
        x_nat = [qa_t.rearrange("p a b -> p (a b)"), big[:, :, :].rearrange("p a b -> p (a b)")]
        sq_junk = k_dup.rearrange("p a b -> p (a b)").rearrange("p (a b) -> p a b", a=2)
        normed_x = [hg[:, 2 * n:2 * n + 2, :].rearrange("p a (b s) -> p (a b) s", b=2) for n in range(2)]
        mask_f = half[:, :, :, :].rearrange("p a b c -> p (a b c)")[:, 0:TAKES * P].rearrange("p (l t) -> p l t", l=TAKES)
        prm, prm_mix = i_nat[:, 0, 0:P], i_nat[:, 1, 0:P]
        x_gain = amax[:, 0, :]
        k_t = i_nat
        sq_acc = hg[:, 0, :].rearrange("p (a b) -> p a b", a=2)
        D, U, KK, QS = (hg[:, n, :] for n in range(4))
        probs = [big[:, c, :].rearrange("p (n k) -> p n k", n=4) for c in range(2)]
        probs_t = [big[:, 2 + c, :].rearrange("p (n k) -> p n k", n=4) for c in range(2)]
        relu_b = [big[:, n, :].rearrange("p (a b) -> p a b", a=2) for n in range(2)]
        sq_b = [big[:, 2 + n, :].rearrange("p (a b) -> p a b", a=2) for n in range(2)]
        y_nat = raw[:, :, :, :].rearrange("p a b c -> p (a b c)").rearrange("p (s n) -> p s n", s=2)
        PIECES = [slice(512 * n, 512 * n + 512) for n in range(3)]
        y_tail = [y_nat[:, :, (N_GROUPS - 2 + n) * COLS:(N_GROUPS - 1 + n) * COLS] for n in range(2)]

        raw_landed = [sem(f"raw_landed{n}") for n in range(UNITS)]
        x_landed = [[sem(f"x_landed{st}{n}") for n in range(4)] for st in range(2)]
        prm_landed = sem("prm_landed")
        mix_landed = sem("mix_landed")
        const_landed = sem("const_landed")
        masks_landed = sem("masks_landed")
        sinks_landed = sem("sinks_landed")
        consts_set = sem("consts_set")
        hi_ready = sem("hi_ready")
        lo_ready = sem("lo_ready")
        unit_used = sem("unit_used")
        half_copied = sem("half_copied")
        acc_free = sem("acc_free")
        dve_step = sem("dve_step")
        cols_turned = sem("cols_turned")
        cols_ready = sem("cols_ready")
        lb_shifted = sem("lb_shifted")
        lb_exp = sem("lb_exp")
        x_turned = sem("x_turned")
        resid_copied = sem("resid_copied")
        ssq_a = sem("ssq_a")
        ssq_v = sem("ssq_v")
        ssq_summed = sem("ssq_summed")
        std_ready = sem("std_ready")
        xrstd_ready = sem("xrstd_ready")
        xdiag_ready = sem("xdiag_ready")
        xrstd_spread = sem("xrstd_spread")
        rstd_copied = sem("rstd_copied")
        in_hi = sem("in_hi")
        in_ready = sem("in_ready")
        masks_set = sem("masks_set")
        gain_staged = sem("gain_staged")
        queries_ready = sem("queries_ready")
        normed = sem("normed")
        normed_hi = sem("normed_hi")
        normed_ready = sem("normed_ready")
        kt_ready = sem("kt_ready")
        k_dup_landed = sem("k_dup_landed")
        staged = sem("staged")
        scores_ready = sem("scores_ready")
        negm_ready = sem("negm_ready")
        exp_ready = sem("exp_ready")
        probs_ready = sem("probs_ready")
        probs_turned = sem("probs_turned")
        probs_copied = sem("probs_copied")
        att_ready = sem("att_ready")
        att_hi = sem("att_hi")
        att_mixed = sem("att_mixed")
        sig_ready = sem("sig_ready")
        gates_ready = sem("gates_ready")
        level_ready = sem("level_ready")
        level_done = sem("level_done")
        level_taken = sem("level_taken")
        cross_copied = sem("cross_copied")
        o_ready = sem("o_ready")
        odiag_ready = sem("odiag_ready")
        orstd_spread = sem("orstd_spread")
        osq_ready = sem("osq_ready")
        oms_ready = sem("oms_ready")
        ostd_ready = sem("ostd_ready")
        o_scaled = sem("o_scaled")
        hg_hi = sem("hg_hi")
        hg_mixed = sem("hg_mixed")
        resid_ready = sem("resid_ready")
        scaled_ready = sem("scaled_ready")
        sq_ready = sem("sq_ready")
        v_hi = sem("v_hi")
        v_ready = sem("v_ready")
        sq_summed = sem("sq_summed")
        ms_ready = sem("ms_ready")
        sq_cleared = sem("sq_cleared")
        mstd_ready = sem("mstd_ready")
        relu_ready = sem("relu_ready")
        hid_sq = sem("hid_sq")
        hid_hi = sem("hid_hi")
        hid_ready = sem("hid_ready")
        fin_sq = sem("fin_sq")
        fin_gained = sem("fin_gained")
        resid_done = sem("resid_done")
        tile_done = sem("tile_done")
        y_copied = sem("y_copied")
        fms_ready = sem("fms_ready")
        fstd_ready = sem("fstd_ready")
        frstd_ready = sem("frstd_ready")
        y_turned = sem("y_turned")
        y_a = sem("y_a")
        y_v = sem("y_v")
        y_stored = sem("y_stored")
        mlp_rstd = sem("mlp_rstd")

        block = ctx.enter_context(nc.Block())

        def x_at(kt):
            return ps[:, 2 + kt // 2 % 6, kt % 2 * SEQ:kt % 2 * SEQ + SEQ]

        def upper_halves(t, l):
            return t.rearrange("p (b two n) -> p b two n", two=2, n=1 << l)[:, :, 1, :]

        def bank_pair(par):
            return ps[:, 2 * par:2 * par + 2, :]

        FIRST_PAIR = [(0, 0), (0, 1)]
        LAST_EVEN = (3, 0)

        def is_group(it, j, k):
            return isinstance(it, int) and 2 * it + j == k

        def last_tiles(it, j):
            return slice(4 * it + 2 * j, 4 * it + 2 * j + 2) if isinstance(it, int) else bass.ds(it * 4 + 2 * j, 2)

        def y_slot(it, j):
            return slice(4 * it + 2 * j - 2, 4 * it + 2 * j) if isinstance(it, int) else bass.ds(it * 4 + (2 * j - 2), 2)

        @block.sync
        def _(sp):
            def load_unit(u, src, row0, col0):
                sp.dma_start(
                    raw[:, u, :, :],
                    src[0, bass.ds(row0 + u * UK * P, UK * P), bass.ds(col0, COLS)].rearrange("(k p) n -> p k n", p=P),
                ).then_inc(raw_landed[u], 16)

            def load(g, par, src, row0, col0):
                for u in range(UNITS):
                    sp.wait_ge(lo_ready, g * UNITS + (u - UNITS + 1))
                    load_unit(u, src, row0, col0)

            sp.dma_start(ident[:, :], identity[:, :]).then_inc(const_landed, 16)
            for n in range(4):
                for st in range(2):
                    sp.dma_start(x_nat[st][:, 512 * n:512 * n + 512],
                                 x[0, st * P:(st + 1) * P, 512 * n:512 * n + 512]).then_inc(x_landed[st][n], 16)
                load_unit(n, w_in, 0, K_A * COLS)
            sp.dma_start(mask_f, level_masks[:, :, :]).then_inc(masks_landed, 16)
            load(G_V, 1, w_in, 0, V_A * COLS)
            with sp.Fori(0, 2) as it:
                for j in range(2):
                    load(it * 2 + (G_QA + j), j, w_in, 0, it * (2 * COLS) + (Q_A + j) * COLS)
            sp.wait_ge(kt_ready, 1)
            for to in range(2):
                for frm in range(2):
                    sp.dma_start(k_dup[to * 64:to * 64 + 64, frm::2, :], k_t[frm * 64:frm * 64 + 64, :, :]).then_inc(k_dup_landed, 16)
            with sp.Fori(0, ITERS) as it:
                for j, part in enumerate((F_H, Q_H, I_H, G_H)):
                    load(it * 4 + (G_HG + j), j % 2, w_in, 0, it * COLS + part * COLS)
            with sp.Fori(0, N_GROUPS // 2) as it:
                for j in range(2):
                    load(it * 2 + (G_OUT + j), j, w_out, 0, it * (2 * COLS) + j * COLS)
            with sp.Fori(0, CHUNKS) as c:
                with sp.Fori(0, N_GROUPS // 2) as it:
                    for j in range(2):
                        load(c * (2 * N_GROUPS) + it * 2 + (G_MLP + j), j, w_up, 0,
                             c * D_MODEL + it * (2 * COLS) + j * COLS)
                with sp.Fori(0, N_GROUPS // 2) as it:
                    for j in range(2):
                        load(c * (2 * N_GROUPS) + it * 2 + (G_MLP + N_GROUPS + j), j, w_down, c * D_MODEL,
                             it * (2 * COLS) + j * COLS)
            for n, piece in enumerate(PIECES):
                for st, ready in ((0, y_v), (1, y_a)):
                    sp.wait_ge(ready, n + 1)
                    sp.dma_start(out[0, st * P:(st + 1) * P, piece], y_nat[:, st, piece]).then_inc(y_stored, 16)
            for n, ready in ((0, y_v), (1, y_a)):
                sp.wait_ge(ready, len(PIECES) + 1)
                at = (N_GROUPS - 2 + n) * COLS
                sp.dma_start(out[0, :, at:at + COLS].rearrange("(s p) n -> p s n", p=P), y_tail[n]).then_inc(y_stored, 16)
            sp.wait_ge(y_stored, (2 * len(PIECES) + 2) * 16)

        @block.gpsimd
        def _(pool):
            nc.gpsimd.memset(ones[:, :], 1.0).then_inc(consts_set, 1)
            nc.gpsimd.memset(eps_c[:, :], EPS).then_inc(consts_set, 1)
            nc.gpsimd.memset(s_t[:, :, :], 0.0).then_inc(consts_set, 1)

            pool.wait_ge(masks_landed, 16)
            nc.gpsimd.tensor_copy(masks[:, :, :], mask_f).then_inc(masks_set, 1)

            def stage(it):
                nc.gpsimd.tensor_copy(k_st[:, :], k_dup[:, bass.ds(it, 1), :].rearrange("p a b -> p (a b)"))
                nc.gpsimd.tensor_copy(q_st[:, :, :], qa_t[:, bass.ds(it * 2, 2), :])
                nc.gpsimd.tensor_copy(v_st[:, :, :], v_all[:, :, bass.ds(it * HEAD_DIM, HEAD_DIM)])
                nc.gpsimd.tensor_copy(sink_st[:, :, :], sink_c[:, :, bass.ds(it * 2, 2)]).then_inc(staged, 1)

            pool.wait_ge(k_dup_landed, 64)
            pool.wait_ge(queries_ready, 1)
            stage(0)
            pool.wait_ge(queries_ready, G_HG - G_QA)
            with pool.Fori(1, ITERS) as it:
                pool.wait_ge(att_ready, it)
                pool.wait_ge(exp_ready, it * 2)
                stage(it)

        CONSTS = 3

        @block.scalar
        def _(act):
            def split(g, par, u, first=False):
                act.wait_ge(raw_landed[u], g * 16 + 16)
                if not first:
                    act.wait_ge(unit_used, g * UNITS + (u + 1 - 2 * UNITS))
                nc.scalar.activation(w_hi[:, par * UNITS + u, :, :], raw[:, u, :, :], ACT.Copy).then_inc(hi_ready, 1)

            def copy_half(g, par):
                act.wait_ge(unit_used, g * UNITS + UNITS)
                nc.scalar.activation(half[:, par, :, :], bank_pair(par)[:, :, SEQ:2 * SEQ], ACT.Copy).then_inc(half_copied, 1)

            act.dma_start(prm_mix[0:KT, :], norm_mix.rearrange("a (t p) -> (a t) p", p=P)).then_inc(mix_landed, 16)
            act.wait_ge(consts_set, CONSTS)
            nc.scalar.activation(stat[:, 7:8], eps_c[:, 0:1], ACT.Sqrt)
            act.wait_ge(cols_ready, 1)

            def copy_resid(u):
                b = 2 + 2 * u % 6
                nc.scalar.activation(resid[:, UK * u:UK * u + UK, :].rearrange("p (a b) s -> p a (b s)", a=2),
                                     ps[:, b:b + 2, :], ACT.Copy).then_inc(resid_copied, 1)

            def square_x(u):
                act.wait_ge(x_landed[0][u], 16)
                nc.scalar.activation(hg[:, u, :], x_nat[0][:, 512 * u:512 * u + 512], ACT.Square,
                                     accum_out=ssq[:, 0, u:u + 1]).then_inc(ssq_a, 1)

            square_x(0)
            for u in range(UNITS):
                act.wait_ge(x_turned, u + 1)
                for kt in range(UK * u, UK * u + UK):
                    last = nc.scalar.activation(act_mid[:, kt, 0:SEQ], x_at(kt), ACT.Copy,
                                                scale=cols[:, C_MIX + kt:C_MIX + kt + 1])
                    if kt % 2 == 1:
                        last.then_inc(in_hi, 1)
                split(G_K, 0, u, first=True)
                if u == 0:
                    for at, src in ((C_MLP, norm_mlp.rearrange("a (t p) -> (a t) p", p=P)),
                                    (C_FIN, final_norm.rearrange("(t p) -> t p", p=P)),
                                    (C_HG, hgrn_norm.rearrange("a (t p) -> (a t) p", p=P)),
                                    (C_LB, lb_logits.rearrange("a (t p) -> (a t) p", p=P))):
                        act.dma_start(prm[at:at + src.shape[0], :], src).then_inc(prm_landed, 16)
                    act.dma_start(sinks_b[:, :], attn_sinks[0:1, :].to_broadcast([P, HEADS])).then_inc(sinks_landed, 16)
                if u == 1:
                    act.wait_ge(in_ready, 1)
                    copy_resid(0)
            act.wait_ge(in_ready, 4)
            copy_resid(3)
            split(G_V, 1, 0, first=True)
            split(G_V, 1, 1, first=True)
            for u in range(1, UNITS):
                square_x(u)
            act.wait_ge(ssq_summed, 1)
            nc.scalar.activation(stat[:, 2:4], stat[:, 0:2], ACT.Sqrt, bias=eps_c[:, 0:1],
                                 scale=1.0 / D_MODEL).then_inc(std_ready, 1)
            copy_resid(1)
            split(G_V, 1, 2, first=True)
            copy_resid(2)
            act.wait_ge(xrstd_spread, 1)
            nc.scalar.activation(rstd[:, :], ps[:, 4, 0:SEQ], ACT.Copy).then_inc(rstd_copied, 1)
            split(G_V, 1, 3, first=True)
            act.wait_ge(masks_set, 1)
            copy_half(G_K, 0)
            split(G_QA, 0, 0)
            split(G_QA, 0, 1)
            act.wait_ge(lb_shifted, 1)
            nc.scalar.activation(lbe[:, 2:4, :], lbe[:, 0:2, :], ACT.Exp).then_inc(lb_exp, 1)
            split(G_QA, 0, 2)
            split(G_QA, 0, 3)
            with act.Fori(0, 2) as it:
                for j in range(2):
                    g = it * 2 + (G_QA + j)
                    split(g + 1, 1 - j, 0)
                    split(g + 1, 1 - j, 1)
                    split(g + 1, 1 - j, 2)
                    act.wait_ge(normed, it * 2 + (j + 1))
                    nc.scalar.activation(act_in[:, bass.ds(it * (2 * UK) + UK * j, UK), 0:SEQ], normed_x[j],
                                         ACT.Copy).then_inc(normed_hi, 1)
                    split(g + 1, 1 - j, 3)
                    copy_half(g, j)

            with act.Fori(0, ITERS) as it:
                g = it * 4 + G_HG

                for u in range(UNITS):
                    split(g + 1, 1, u)
                copy_half(g, 0)
                for c in range(2):
                    act.wait_ge(negm_ready, it * 2 + (c + 1))
                    for n in range(N_CHUNKS):
                        w = CHUNK if n == 0 else 2 * CHUNK
                        nc.scalar.activation(probs[c][:, n, 0:w], ps[:, 4 + c, n * P:n * P + w], ACT.Exp,
                                             bias=negm[:, c, n:n + 1], scale=SCALE,
                                             accum_out=asum[:, c, n:n + 1])
                    nc.scalar.activation(esink[:, c, :], negm[:, c, :], ACT.Exp,
                                         bias=sink_st[:, 0, c:c + 1]).then_inc(exp_ready, 1)
                act.wait_ge(acc_free, g + 1)
                nc.scalar.activation(sig[:, :], half[:, 0, :, :].rearrange("p a b -> p (a b)"), ACT.Sigmoid).then_inc(sig_ready, 1)

                for u in range(UNITS):
                    split(g + 2, 0, u)
                    if u == 2:
                        for c in range(2):
                            act.wait_ge(probs_turned, it * 2 + (c + 1))
                            nc.scalar.activation(probs_t[c][0:CHUNK, 0, :], ps[0:CHUNK, 6 + c, 0:P], ACT.Copy)
                            nc.scalar.activation(probs_t[c][:, 1:4, :],
                                                 ps[:, 6 + c, P:4 * P].rearrange("p (n k) -> p n k", n=3),
                                                 ACT.Copy).then_inc(probs_copied, 1)
                copy_half(g + 1, 1)
                act.wait_ge(acc_free, g + 2)
                act.wait_ge(gates_ready, it * 2 + 1)
                nc.scalar.activation(sig[:, :], half[:, 1, :, :].rearrange("p a b -> p (a b)"), ACT.Sigmoid).then_inc(sig_ready, 1)
                act.wait_ge(att_ready, it + 1)
                nc.scalar.activation(act_mid[:, bass.ds(it * 2, 2), 0:SEQ], ps[:, 4:6, 0:SEQ], ACT.Copy).then_inc(att_hi, 1)

                for u in range(UNITS):
                    split(g + 3, 1, u)

                split(g + 4, 0, 0)
                split(g + 4, 0, 1)
                act.wait_ge(level_done, it * 8 + 8)
                nc.scalar.activation(s_x[:, :, :], ps[:, 7, SEQ:2 * SEQ].rearrange("p (h t) -> p h t", h=2), ACT.Copy)
                act.wait_ge(level_taken, it * TAKES + TAKES)
                nc.scalar.activation(s_t[0:64, :, 64:128], ps[0:64, 7, 0:SEQ].rearrange("p (a b) -> p a b", a=4), ACT.Copy)
                for s0 in (0, 64):
                    last = nc.scalar.activation(
                        s_t[s0:s0 + 32, :, s0 + 32:s0 + 64],
                        ps[s0:s0 + 32, 6, :].rearrange("p (a b) -> p a b", a=4)[:, :, s0 // 2:s0 // 2 + 32], ACT.Copy)
                last.then_inc(cross_copied, 1)
                split(g + 4, 0, 2)
                act.wait_ge(o_ready, it + 1)
                nc.scalar.activation(big[:, 0, :], ps[:, 7, :], ACT.Square).then_inc(osq_ready, 1)
                nc.scalar.activation(big[:, 2, :], ps[:, 7, :], ACT.Copy)
                act.wait_ge(oms_ready, it + 1)
                nc.scalar.activation(stat[:, 0:4], ps[:, 6, 0:4], ACT.Sqrt, bias=eps_c[:, 0:1], scale=1.0 / P).then_inc(ostd_ready, 1)
                split(g + 4, 0, 3)
                copy_half(g + 3, 1)
                act.wait_ge(acc_free, g + 4)
                nc.scalar.activation(sig[:, :], half[:, 1, :, :].rearrange("p a b -> p (a b)"), ACT.Sigmoid).then_inc(sig_ready, 1)
                act.wait_ge(o_scaled, it + 1)
                nc.scalar.activation(act_mid[:, bass.ds(it * 2 + 8, 2), 0:SEQ],
                                     big[:, 0, :].rearrange("p (h t) -> p h t", h=2), ACT.Copy).then_inc(hg_hi, 1)

            with act.Fori(0, N_GROUPS // 2) as it:
                for j in range(2):
                    g = it * 2 + (G_OUT + j)
                    for u in range(UNITS):
                        split(g + 1, 1 - j, u)
                    copy_half(g, j)
                    act.wait_ge(resid_ready, it * 2 + (j + 1))
                    nc.scalar.activation(sq_b[j], resid[:, bass.ds(it * 4 + 2 * j, 2), :], ACT.Square).then_inc(sq_ready, 1)
                    act.wait_ge(scaled_ready, it * 2 + (j + 1))
                    nc.scalar.activation(act_in[:, bass.ds(it * 4 + 2 * j, 2), 0:SEQ], relu_b[j], ACT.Copy).then_inc(v_hi, 1)
            act.wait_ge(ms_ready, 1)
            nc.scalar.activation(sig[:, SEQ:2 * SEQ], ps[:, 4, 0:SEQ], ACT.Sqrt, bias=eps_c[:, 0:1],
                                 scale=1.0 / D_MODEL).then_inc(mstd_ready, 1)

            def up_step(g, j, n, k):
                for u in range(UNITS):
                    split(g + 1, 1 - j, u)
                copy_half(g, j)
                act.wait_ge(relu_ready, k + 1)
                nc.scalar.activation(sq_b[j], relu_b[j], ACT.Square).then_inc(hid_sq, 1)
                act.wait_ge(hid_sq, k + 1)
                nc.scalar.activation(act_mid[:, bass.ds(n, 2), 0:SEQ], sq_b[j], ACT.Copy).then_inc(hid_hi, 1)

            def chunk(c, last):
                g0 = c * (2 * N_GROUPS) + G_MLP
                with act.Fori(0, N_GROUPS // 2) as it:
                    for j in range(2):
                        up_step(it * 2 + g0 + j, j, it * 4 + 2 * j, c * N_GROUPS + it * 2 + j)
                if not last:
                    with act.Fori(0, N_GROUPS // 2) as it:
                        for j in range(2):
                            g = it * 2 + g0 + (N_GROUPS + j)
                            for u in range(UNITS):
                                split(g + 1, 1 - j, u)
                            copy_half(g, j)

            def last_down(it, j):
                k = it * 2 + j
                g = it * 2 + (G_END - N_GROUPS + j)
                for u in range(UNITS):
                    split(g + 1, 1 - j, u)
                if not is_group(it, j, 0):
                    act.wait_ge(y_turned, k)
                    nc.scalar.activation(qk[:, y_slot(it, j), :], ps[:, 5 - j, :].rearrange("p (s n) -> p s n", s=2),
                                         ACT.Copy).then_inc(y_copied, 1)
                copy_half(g, j)
                act.wait_ge(resid_done, k + 1)
                nc.scalar.activation(sq_b[j], resid[:, last_tiles(it, j), :], ACT.Square).then_inc(fin_sq, 1)

            with act.Fori(0, CHUNKS - 1) as c:
                chunk(c, 0)
            chunk(CHUNKS - 1, 1)
            for it, j in FIRST_PAIR:
                last_down(it, j)
            with act.Fori(1, N_GROUPS // 2 - 1) as it:
                for j in range(2):
                    last_down(it, j)
            last_down(*LAST_EVEN)
            for b in range(2):
                act.wait_ge(resid_done, N_GROUPS + b)
                nc.scalar.activation(sq_b[1][:, b, :], resid[:, KT - 2 + b, :], ACT.Square).then_inc(fin_sq, 1)

            act.wait_ge(fms_ready, 1)
            nc.scalar.activation(stat[:, 0:2], ps[:, 6:8, 0:1].rearrange("p a b -> p (a b)"), ACT.Sqrt, bias=eps_c[:, 0:1],
                                 scale=1.0 / D_MODEL).then_inc(fstd_ready, 1)
            act.wait_ge(frstd_ready, 1)
            for n in range(len(PIECES)):
                nc.scalar.activation(y_nat[:, 1, PIECES[n]].rearrange("p (k n) -> p k n", k=2),
                                     qk[:, 4 * n + 1:4 * n + 4:2, :], ACT.Copy, scale=stat[:, 3:4]).then_inc(y_a, 1)
            act.wait_ge(y_turned, N_GROUPS)
            for st in range(2):
                last = nc.scalar.activation(y_tail[1][:, st, :], ps[:, 5, st * SEQ:st * SEQ + SEQ], ACT.Copy,
                                            scale=stat[:, 2 + st:3 + st])
            last.then_inc(y_a, 1)

        @block.vector
        def _(dve):
            vec = nc.vector

            def split(g, par, u):
                dve.wait_ge(hi_ready, g * UNITS + (u + 1))
                s = par * UNITS + u
                vec.tensor_tensor(w_lo[:, s, :, :], raw[:, u, :, :], w_hi[:, s, :, :].bitcast(F32),
                                  ALU.subtract).then_inc(lo_ready, 1)

            def sum_half(g, par, halves, to=None):
                dve.wait_ge(half_copied, halves)
                to = half[:, par, :, :] if to is None else to
                vec.tensor_tensor(to, bank_pair(par)[:, :, 0:SEQ], half[:, par, :, :], ALU.add).then_inc(acc_free, 1)

            steps = [0]

            def link(ins, base=None):
                steps[0] += 1
                ins.then_inc(dve_step, 1)
                dve.wait_ge(dve_step, steps[0] if base is None else base + steps[0])

            dve.wait_ge(cols_turned, 1)
            vec.tensor_copy(cols[:, C_MIX:C_MIX + KT], ps[:, 1, 0:KT]).then_inc(cols_ready, 1)
            dve.wait_ge(cols_ready, 1)
            def square_x(u):
                dve.wait_ge(x_landed[1][u], 16)
                if u >= 2:
                    dve.wait_ge(ssq_v, u - 1)
                vec.tensor_tensor_reduce(sq_junk[:, u % 2, :], x_nat[1][:, 512 * u:512 * u + 512],
                                         x_nat[1][:, 512 * u:512 * u + 512], 1.0, 0.0, ALU.mult, ALU.add,
                                         ssq[:, 1, u:u + 1]).then_inc(ssq_v, 1)

            square_x(0)
            for u in range(UNITS):
                for kt in range(UK * u, UK * u + UK):
                    if kt % 2 == 0:
                        dve.wait_ge(in_hi, kt // 2 + 1)
                    last = vec.scalar_tensor_tensor(out=act_mid[:, kt, SEQ:2 * SEQ], in0=x_at(kt),
                                                    scalar=cols[:, C_MIX + kt:C_MIX + kt + 1],
                                                    in1=act_mid[:, kt, 0:SEQ].bitcast(F32),
                                                    op0=ALU.mult, op1=ALU.subtract)
                last.then_inc(in_ready, 1)
                split(G_K, 0, u)
            split(G_V, 1, 0)
            split(G_V, 1, 1)
            for u in range(1, UNITS):
                square_x(u)
            dve.wait_ge(ssq_a, UNITS)
            dve.wait_ge(ssq_v, UNITS)
            vec.tensor_reduce(stat[:, 0:2], ssq[:, :, :], AX.X, ALU.add).then_inc(ssq_summed, 1)
            dve.wait_ge(std_ready, 1)
            vec.reciprocal(stat[:, 4:6], stat[:, 2:4]).then_inc(xrstd_ready, 1)
            dve.wait_ge(xrstd_ready, 1)
            vec.tensor_tensor(s_x[:, :, :], ident[:, :].unsqueeze(1).to_broadcast([P, 2, P]),
                              stat[:, 4:6].unsqueeze(2).to_broadcast([P, 2, P]), ALU.mult).then_inc(xdiag_ready, 1)
            split(G_V, 1, 2)
            split(G_V, 1, 3)

            dve.wait_ge(cols_turned, 2)
            vec.tensor_copy(cols[:, 0:C_MIX], ps[:, 5, 0:C_MIX]).then_inc(cols_ready, 1)
            dve.wait_ge(half_copied, 1)
            vec.tensor_tensor(half[:, 0, :, :], bank_pair(0)[:, :, 0:SEQ], half[:, 0, :, :], ALU.add).then_inc(acc_free, 1)
            dve.wait_ge(acc_free, 1)
            dve.wait_ge(rstd_copied, 1)
            vec.tensor_tensor(k_t[:, :, :], half[:, 0, :, :], rstd[:, :].unsqueeze(1).to_broadcast([P, 2, SEQ]),
                              ALU.mult).then_inc(kt_ready, 1)
            split(G_QA, 0, 0)
            split(G_QA, 0, 1)
            dve.wait_ge(cols_ready, 2)
            l0, l1 = cols[:, C_LB:C_LB + 8], cols[:, C_LB + 8:C_LB + 16]
            link(vec.tensor_tensor(lbe[:, 2, :], l0, l1, ALU.max))
            vec.tensor_tensor(lbe[:, 0, :], l0, lbe[:, 2, :], ALU.subtract)
            vec.tensor_tensor(lbe[:, 1, :], l1, lbe[:, 2, :], ALU.subtract).then_inc(lb_shifted, 1)
            dve.wait_ge(lb_exp, 1)
            link(vec.tensor_tensor(lbe[:, 0, :], lbe[:, 2, :], lbe[:, 3, :], ALU.add))
            link(vec.reciprocal(lbe[:, 1, :], lbe[:, 0, :]))
            link(vec.tensor_tensor(lbc[:, 0, :], lbe[:, 2, :], lbe[:, 1, :], ALU.mult))
            link(vec.tensor_scalar(lbc[:, 1, :], lbc[:, 0, :], -1.0, 1.0, ALU.mult, ALU.add))
            dve.wait_ge(sinks_landed, 16)
            for h in range(2):
                vec.tensor_copy(sink_c[64 * h:64 * h + 64, 0, :], sinks_b[64 * h:64 * h + 64, h::2])
                last = vec.tensor_scalar(sink_c[64 * h:64 * h + 64, 1, :], sinks_b[64 * h:64 * h + 64, h::2], -1.0, None, ALU.mult)
            link(last)
            split(G_QA, 0, 2)
            split(G_QA, 0, 3)
            dve.wait_ge(unit_used, (G_V + 1) * UNITS)
            for st in range(2):
                vec.tensor_scalar(v_all[:, st, :], ps[:, 2 + st, 0:COLS], stat[:, 4 + st:5 + st], None, ALU.mult)
            vec.tensor_scalar(v_all[0:64, 2, :], ps[0:64, 3, 0:COLS], stat[0:64, 5:6], None, ALU.mult)
            vec.tensor_scalar(v_all[64:128, 2, :], ps[64:128, 2, 0:COLS], stat[64:128, 4:5], None, ALU.mult).then_inc(acc_free, 1)
            dve.wait_ge(resid_copied, UNITS)
            dve.wait_ge(x_turned, UNITS)
            with dve.Fori(0, 2) as it:
                for j in range(2):
                    g = it * 2 + (G_QA + j)
                    n = it * 2 + (j + 1)
                    kt = it * (2 * UK) + UK * j
                    split(g + 1, 1 - j, 0)
                    split(g + 1, 1 - j, 1)
                    vec.tensor_copy(x_gain, cols[:, bass.ds(kt + C_MIX, UK)]).then_inc(gain_staged, 1)
                    dve.wait_ge(gain_staged, n)
                    for t in range(UK):
                        last = vec.scalar_tensor_tensor(out=normed_x[j][:, t, :],
                                                        in0=resid[:, bass.ds(kt + t, 1), :].rearrange("p a b -> p (a b)"),
                                                        scalar=x_gain[:, t:t + 1], in1=rstd[:, :],
                                                        op0=ALU.mult, op1=ALU.mult)
                    last.then_inc(normed, 1)
                    split(g + 1, 1 - j, 2)
                    dve.wait_ge(normed_hi, n)
                    vec.tensor_tensor(act_in[:, bass.ds(kt, UK), SEQ:2 * SEQ], normed_x[j],
                                      act_in[:, bass.ds(kt, UK), 0:SEQ].bitcast(F32), ALU.subtract).then_inc(normed_ready, 1)
                    split(g + 1, 1 - j, 3)
                    sum_half(g, j, it * 2 + (j + 2))
                    dve.wait_ge(acc_free, g + 1)
                    vec.tensor_tensor(qa_t[:, bass.ds(it * 4 + 2 * j, 2), :], half[:, j, :, :],
                                      rstd[:, :].unsqueeze(1).to_broadcast([P, 2, SEQ]), ALU.mult).then_inc(queries_ready, 1)
            dve.wait_ge(acc_free, G_HG)
            dve.wait_ge(masks_set, 1)

            def levels_view(t, n):
                return t.rearrange("p (b two n) -> p b two n", two=2, n=n)

            PER_ITER = 24
            pre = steps[0]
            with dve.Fori(0, ITERS) as it:
                steps[0] = pre
                base = it * PER_ITER
                g = it * 4 + G_HG
                lv = it * 8
                n_e = it * 8

                vec.tensor_copy(lb_st[:, :, :], lbc[:, :, bass.ds(it * 2, 2)])
                vec.tensor_copy(gain_st[:, :], cols[:, bass.ds(it * 2 + C_HG, 2)])
                for u in range(UNITS):
                    split(g + 1, 1, u)
                dve.wait_ge(staged, it + 1)
                for c in range(2):
                    dve.wait_ge(scores_ready, it * 2 + (c + 1))
                    link(vec.tensor_reduce(amax[:, c, :], ps[:, 4 + c, :].rearrange("p (n k) -> p n k", n=4),
                                           AX.X, ALU.max), base)
                    vec.tensor_scalar(negm[:, c, :], amax[:, c, :], -SCALE, sink_st[:, 1, c:c + 1],
                                      ALU.mult, ALU.min).then_inc(negm_ready, 1)
                sum_half(g, 0, it * 3 + 6)
                for c in range(2):
                    dve.wait_ge(exp_ready, it * 2 + (c + 1))
                    link(vec.tensor_tensor(asum[:, c, :], asum[:, c, :], esink[:, c, :], ALU.add), base)
                    link(vec.reciprocal(esink[:, c, :], asum[:, c, :]), base)
                    vec.tensor_scalar(probs[c][:, 0, 0:CHUNK], probs[c][:, 0, 0:CHUNK], esink[:, c, 0:1], None, ALU.mult)
                    vec.tensor_tensor(probs[c][:, 1:4, :], probs[c][:, 1:4, :],
                                      esink[:, c, 1:4].unsqueeze(2).to_broadcast([P, 3, P]), ALU.mult).then_inc(probs_ready, 1)
                dve.wait_ge(sig_ready, it * 3 + 1)
                for h in range(2):
                    sl = slice(h * SEQ, h * SEQ + SEQ)
                    last = vec.tensor_scalar(D[:, sl], sig[:, sl], lb_st[:, 1, h:h + 1], lb_st[:, 0, h:h + 1], ALU.mult, ALU.add)
                last.then_inc(gates_ready, 1)
                dve.wait_ge(gates_ready, it * 2 + 1)
                link(vec.tensor_scalar(KK, D, -1.0, 1.0, ALU.mult, ALU.add), base)

                for u in range(UNITS):
                    split(g + 2, 0, u)
                sum_half(g + 1, 1, it * 3 + 7)
                dve.wait_ge(sig_ready, it * 3 + 2)
                dve.wait_ge(acc_free, g + 2)
                vec.tensor_tensor(QS, half[:, 1, :, :].rearrange("p a b -> p (a b)"), sig[:, :], ALU.mult).then_inc(gates_ready, 1)
                dve.wait_ge(gates_ready, it * 2 + 2)

                def settle():
                    dve.wait_ge(dve_step, base + steps[0])

                def mark(ins):
                    steps[0] += 1
                    ins.then_inc(dve_step, 1)

                def operand(l):
                    n = 1 << l
                    E = levels_view(big[:, l % 4, :], n)
                    d, uu, kk, qq = (levels_view(t, n) for t in (D, U, KK, QS))
                    if l:
                        settle()
                    if l >= 4:
                        dve.wait_ge(level_done, lv + (l - 4 + 2))
                    if l == 0:
                        vec.tensor_copy(E[:, :, 0, :], kk[:, :, 0, :])
                    else:
                        vec.tensor_tensor(E[:, :, 0, :], kk[:, :, 0, :], uu[:, :, 0, :], ALU.mult)
                    vec.tensor_tensor(E[:, :, 1, :], qq[:, :, 1, :], d[:, :, 1, :], ALU.mult).then_inc(level_ready, 1)

                def extend_u(l):
                    n = 1 << l
                    d, uu = levels_view(D, n), levels_view(U, n)
                    if l == 0:
                        vec.memset(uu[:, :, 1, :], 1.0)
                        mark(vec.tensor_copy(uu[:, :, 0, :], d[:, :, 1, :]))
                    else:
                        mark(vec.tensor_tensor(uu[:, :, 0, :], uu[:, :, 0, :],
                                               d[:, :, 1, n - 1:n].to_broadcast([P, 512 // (2 * n), n]), ALU.mult))

                def extend_d(l):
                    n = 1 << l
                    d = levels_view(D, n)
                    settle()
                    mark(vec.tensor_tensor(d[:, :, 1, :], d[:, :, 1, :],
                                           d[:, :, 0, n - 1:n].to_broadcast([P, 512 // (2 * n), n]), ALU.mult))

                def take(i):
                    dve.wait_ge(level_done, lv + (i + 1))
                    if i:
                        dve.wait_ge(level_taken, it * TAKES + i)
                    vec.memset(wait_mark[:, i:i + 1], 0.0)
                    if i == 0:
                        to, mask = s_t[:, :, :], masks[:, 0:1, :].to_broadcast([P, 4, P])
                        scored = ps[:, 4, :].rearrange("p (a t) -> p a t", a=4)
                    else:
                        n = 1 << (i - 1)
                        to = s_t[:, :, :].rearrange("p a (b two n) -> p a b two n", two=2, n=n)[:, :, :, 1, :]
                        mask = upper_halves(masks[:, i, :], i - 1).unsqueeze(1).to_broadcast([P, 4, 64 // n, n])
                        scored = ps[:, 4 + i % 4, :].rearrange("p (a c b n) -> p a c b n", a=4, c=2, n=n)[:, :, 0, :, :]
                    vec.copy_predicated(to, mask, scored).then_inc(level_taken, 1)

                operand(0)
                extend_u(0)
                dve.wait_ge(att_hi, it + 1)
                at = act_mid[:, bass.ds(it * 2, 2), :]
                vec.tensor_tensor(at[:, :, SEQ:2 * SEQ], ps[:, 4:6, 0:SEQ], at[:, :, 0:SEQ].bitcast(F32),
                                  ALU.subtract).then_inc(att_mixed, 1)
                extend_d(0)
                operand(1)
                extend_u(1)
                split(g + 3, 1, 0)
                extend_d(1)
                operand(2)
                extend_u(2)
                split(g + 3, 1, 1)
                extend_d(2)
                operand(3)
                extend_u(3)
                take(0)
                extend_d(3)
                take(1)
                operand(4)
                extend_u(4)
                take(2)
                extend_d(4)
                operand(5)
                extend_u(5)
                take(3)
                extend_d(5)
                operand(6)
                extend_u(6)
                split(g + 3, 1, 2)
                extend_d(6)
                operand(7)
                take(4)
                dve.wait_ge(unit_used, g * UNITS + 3 * UNITS)
                vec.tensor_copy(i_nat[:, :, :], bank_pair(0)[:, :, 0:COLS]).then_inc(acc_free, 1)
                take(5)
                split(g + 3, 1, 3)

                split(g + 4, 0, 0)
                split(g + 4, 0, 1)
                split(g + 4, 0, 2)
                dve.wait_ge(ostd_ready, it + 1)
                link(vec.reciprocal(stat[:, 4:8], stat[:, 0:4]), base)
                vec.tensor_tensor(big[:, 1, :].rearrange("p (n t) -> p n t", n=4),
                                  ident[:, :].unsqueeze(1).to_broadcast([P, 4, P]),
                                  stat[:, 4:8].unsqueeze(2).to_broadcast([P, 4, P]), ALU.mult).then_inc(odiag_ready, 1)
                split(g + 4, 0, 3)
                dve.wait_ge(orstd_spread, it + 1)
                for h in range(2):
                    sl = slice(h * SEQ, h * SEQ + SEQ)
                    last = vec.scalar_tensor_tensor(out=big[:, 3, sl], in0=ps[:, 6, sl], scalar=gain_st[:, h:h + 1],
                                                    in1=big[:, 2, sl], op0=ALU.mult, op1=ALU.mult)
                link(last, base)
                sum_half(g + 3, 1, it * 3 + 8)
                dve.wait_ge(acc_free, g + 4)
                link(vec.tensor_tensor(big[:, 3, :], half[:, 1, :, :].rearrange("p a b -> p (a b)"), big[:, 3, :], ALU.mult), base)
                dve.wait_ge(sig_ready, it * 3 + 3)
                vec.tensor_tensor(big[:, 0, :], big[:, 3, :], sig[:, :], ALU.mult).then_inc(o_scaled, 1)
                dve.wait_ge(hg_hi, it + 1)
                at = act_mid[:, bass.ds(it * 2 + 8, 2), :]
                vec.tensor_tensor(at[:, :, SEQ:2 * SEQ], big[:, 0, :].rearrange("p (h t) -> p h t", h=2),
                                  at[:, :, 0:SEQ].bitcast(F32), ALU.subtract).then_inc(hg_mixed, 1)
                PER = steps[0] - pre
            assert PER == PER_ITER, PER
            HALVES = 1 + 4 + 3 * ITERS
            after = PER_ITER * ITERS - PER_ITER

            link(vec.memset(sq_acc, 0.0), after)
            with dve.Fori(0, N_GROUPS // 2) as it:
                for j in range(2):
                    g = it * 2 + (G_OUT + j)
                    for u in range(UNITS):
                        split(g + 1, 1 - j, u)
                    sum_half(g, j, it * 2 + (HALVES + j + 1))
                    dve.wait_ge(acc_free, g + 1)
                    tiles = bass.ds(it * 4 + 2 * j, 2)
                    vec.tensor_tensor(resid[:, tiles, :], resid[:, tiles, :], half[:, j, :, :], ALU.add).then_inc(resid_ready, 1)
                    dve.wait_ge(resid_ready, it * 2 + (j + 1))
                    vec.tensor_tensor(relu_b[j], resid[:, tiles, :],
                                      cols[:, bass.ds(it * 4 + (C_MLP + 2 * j), 2)].unsqueeze(2).to_broadcast([P, 2, SEQ]),
                                      ALU.mult).then_inc(scaled_ready, 1)
                    dve.wait_ge(sq_ready, it * 2 + (j + 1))
                    vec.tensor_tensor(sq_acc, sq_acc, sq_b[j], ALU.add).then_inc(sq_summed, 1)
                    dve.wait_ge(v_hi, it * 2 + (j + 1))
                    vec.tensor_tensor(act_in[:, tiles, SEQ:2 * SEQ], relu_b[j], act_in[:, tiles, 0:SEQ].bitcast(F32),
                                      ALU.subtract).then_inc(v_ready, 1)
                    dve.wait_ge(sq_summed, it * 2 + (j + 1))
            HALVES2 = HALVES + N_GROUPS
            dve.wait_ge(mstd_ready, 1)
            vec.reciprocal(rstd[:, :], sig[:, SEQ:2 * SEQ]).then_inc(mlp_rstd, 1)
            vec.memset(sq_acc, 0.0).then_inc(sq_cleared, 1)
            dve.wait_ge(mlp_rstd, 1)

            def chunk(c, last):
                g0 = c * (2 * N_GROUPS) + G_MLP
                h0 = c * (2 * N_GROUPS) + HALVES2
                with dve.Fori(0, N_GROUPS // 2) as it:
                    for j in range(2):
                        g = it * 2 + g0 + j
                        k = c * N_GROUPS + it * 2 + j
                        for u in range(UNITS):
                            split(g + 1, 1 - j, u)
                        sum_half(g, j, it * 2 + h0 + (j + 1))
                        dve.wait_ge(acc_free, g + 1)
                        for t in range(2):
                            last_i = vec.scalar_tensor_tensor(out=relu_b[j][:, t, :], in0=half[:, j, t, :], scalar=0.0,
                                                              in1=rstd[:, :], op0=ALU.max, op1=ALU.mult)
                        last_i.then_inc(relu_ready, 1)
                        dve.wait_ge(hid_hi, k + 1)
                        tiles = bass.ds(it * 4 + 2 * j, 2)
                        vec.tensor_tensor(act_mid[:, tiles, SEQ:2 * SEQ], sq_b[j], act_mid[:, tiles, 0:SEQ].bitcast(F32),
                                          ALU.subtract).then_inc(hid_ready, 1)

                if not last:
                    with dve.Fori(0, N_GROUPS // 2) as it:
                        for j in range(2):
                            g = it * 2 + g0 + (N_GROUPS + j)
                            for u in range(UNITS):
                                split(g + 1, 1 - j, u)
                            sum_half(g, j, it * 2 + h0 + (N_GROUPS + j + 1))
                            dve.wait_ge(acc_free, g + 1)
                            tiles = bass.ds(it * 4 + 2 * j, 2)
                            vec.tensor_tensor(resid[:, tiles, :], resid[:, tiles, :], half[:, j, :, :], ALU.add)

            def last_down(it, j):
                k = it * 2 + j
                g = it * 2 + (G_END - N_GROUPS + j)
                for u in range(UNITS):
                    split(g + 1, 1 - j, u)
                sum_half(g, j, it * 2 + (HALVES2 + CHUNKS * 2 * N_GROUPS - N_GROUPS + j + 1))
                dve.wait_ge(acc_free, g + 1)
                tiles = last_tiles(it, j)
                vec.tensor_tensor(resid[:, tiles, :], resid[:, tiles, :], half[:, j, :, :], ALU.add).then_inc(resid_done, 1)
                dve.wait_ge(resid_done, k + 1)
                if not (is_group(it, j, 0) or is_group(it, j, 1)):
                    dve.wait_ge(y_turned, k - 1)
                gains = slice(C_FIN + 4 * it + 2 * j, C_FIN + 4 * it + 2 * j + 2) if isinstance(it, int) \
                    else bass.ds(it * 4 + (C_FIN + 2 * j), 2)
                vec.tensor_tensor(relu_b[j], resid[:, tiles, :], cols[:, gains].unsqueeze(2).to_broadcast([P, 2, SEQ]),
                                  ALU.mult).then_inc(fin_gained, 1)
                dve.wait_ge(fin_sq, k + 1)
                dve.wait_ge(sq_cleared, k + 1)
                vec.tensor_tensor(sq_acc, sq_acc, sq_b[j], ALU.add).then_inc(sq_cleared, 1)

            with dve.Fori(0, CHUNKS - 1) as c:
                chunk(c, 0)
            chunk(CHUNKS - 1, 1)
            for it, j in FIRST_PAIR:
                last_down(it, j)
            with dve.Fori(1, N_GROUPS // 2 - 1) as it:
                for j in range(2):
                    last_down(it, j)
            last_down(*LAST_EVEN)
            for b in range(2):
                dve.wait_ge(tile_done, b + 1)
                tile = resid[:, KT - 2 + b, :]
                vec.tensor_tensor(tile, ps[:, 2 + b, 0:SEQ], tile, ALU.add).then_inc(resid_done, 1)
                dve.wait_ge(resid_done, N_GROUPS + b)
                dve.wait_ge(y_turned, N_GROUPS - 2)
                vec.tensor_scalar(relu_b[1][:, b, :], tile, cols[:, C_FIN + KT - 2 + b:C_FIN + KT - 1 + b], None,
                                  ALU.mult).then_inc(fin_gained, 1)

            dve.wait_ge(fstd_ready, 1)
            vec.reciprocal(stat[:, 2:4], stat[:, 0:2]).then_inc(frstd_ready, 1)
            dve.wait_ge(frstd_ready, 1)
            dve.wait_ge(y_copied, N_GROUPS - 2)
            for n in range(len(PIECES)):
                vec.tensor_scalar(y_nat[:, 0, PIECES[n]].rearrange("p (k n) -> p k n", k=2),
                                  qk[:, 4 * n:4 * n + 4:2, :], stat[:, 2:3], None, ALU.mult).then_inc(y_v, 1)
            dve.wait_ge(y_turned, N_GROUPS - 1)
            for st in range(2):
                last = vec.tensor_scalar(y_tail[0][:, st, :], ps[:, 4, st * SEQ:st * SEQ + SEQ], stat[:, 2 + st:3 + st],
                                         None, ALU.mult)
            last.then_inc(y_v, 1)

        @block.tensor
        def _(pe):
            mm = nc.tensor.matmul

            def unit(g, par, u, acts, natural=False, first=False):
                if u == 0 and not first:
                    pe.wait_ge(acc_free, g - 1)
                pe.wait_ge(lo_ready, g * UNITS + (u + 1))
                for t in range(UK):
                    kt = UK * u + t
                    hi, lo = w_hi[:, par * UNITS + u, t, :], w_lo[:, par * UNITS + u, t, :]
                    one, end = kt == 0, kt == KT - 1
                    for b in range(2):
                        part = slice(b * P, b * P + P)
                        if natural:
                            to = ps[:, 2 * par + b, 0:COLS]
                            a_hi, a_lo = acts[:, kt, b * P:b * P + P], acts[:, kt, SEQ + b * P:SEQ + b * P + P]
                            mm(to, a_hi, hi, start=one, stop=False)
                            mm(to, a_hi, lo, start=False, stop=False)
                            last = mm(to, a_lo, hi, start=False, stop=end)
                        else:
                            mm(ps[:, 2 * par + b, :], hi[:, part], acts[:, kt, :], start=one, stop=False)
                            last = mm(ps[:, 2 * par + b, 0:SEQ], lo[:, part], acts[:, kt, 0:SEQ], start=False, stop=end)
                last.then_inc(unit_used, 1)

            def keep_busy(n):
                for _ in range(n):
                    mm(ps[:, 0, 0:P], ones[:, :], ones[:, :], start=True, stop=True)

            pe.wait_ge(consts_set, 1)
            keep_busy(10)
            pe.wait_ge(const_landed, 16)
            pe.wait_ge(mix_landed, 16)
            pe.transpose(ps[:, 1, 0:KT], prm_mix[0:KT, :], ident[0:KT, 0:KT]).then_inc(cols_turned, 1)

            def turn_x(u):
                pe.wait_ge(x_landed[0][u], 16)
                pe.wait_ge(x_landed[1][u], 16)
                for kt in range(UK * u, UK * u + UK):
                    for st in range(2):
                        last = pe.transpose(x_at(kt)[:, st * P:st * P + P], x_nat[st][:, kt * P:kt * P + P], ident[:, :])
                last.then_inc(x_turned, 1)

            turn_x(0)
            keep_busy(4)
            turn_x(1)
            keep_busy(8)
            turn_x(2)
            pe.wait_ge(in_ready, 1)
            unit(G_K, 0, 0, act_mid, first=True)
            pe.wait_ge(resid_copied, 1)
            turn_x(3)
            for u in range(1, UNITS):
                pe.wait_ge(in_ready, u + 1)
                unit(G_K, 0, u, act_mid, first=True)
            pe.wait_ge(resid_copied, 2)
            unit(G_V, 1, 0, act_mid, natural=True, first=True)
            unit(G_V, 1, 1, act_mid, natural=True, first=True)
            pe.wait_ge(resid_copied, 3)
            pe.wait_ge(xdiag_ready, 1)
            mm(ps[:, 4, 0:SEQ], ones[:, :], s_x[:, :, :].rearrange("p a b -> p (a b)"), start=True, stop=True).then_inc(xrstd_spread, 1)
            pe.wait_ge(prm_landed, 4 * 16)
            pe.transpose(ps[:, 5, 0:C_MIX], prm[0:C_MIX, :], ident[0:C_MIX, 0:C_MIX]).then_inc(cols_turned, 1)
            for u in range(2, UNITS):
                unit(G_V, 1, u, act_mid, natural=True, first=True)
            with pe.Fori(0, 2) as it:
                for j in range(2):
                    for u in range(UNITS):
                        unit(it * 2 + (G_QA + j), j, u, act_mid)
            pe.wait_ge(normed_ready, UNITS - 1)

            with pe.Fori(0, ITERS) as it:
                g = it * 4 + G_HG

                def scores():
                    for c in range(2):
                        for n in range(N_CHUNKS):
                            spans = {0: [(0, 0, 64), (64, 0, 64)], 1: [(0, 0, 128)],
                                     2: [(0, 128, 64), (64, 64, 64)], 3: [(0, 128, 128)]}[n]
                            for h in range(2):
                                hs = slice(64 * h, 64 * h + 64)
                                for at, key, w in spans:
                                    last = mm(ps[hs, 4 + c, n * P + at:n * P + at + w],
                                              q_st[hs, c, n * CHUNK:n * CHUNK + CHUNK],
                                              k_st[hs, key:key + w], start=True, stop=True)
                        last.then_inc(scores_ready, 1)

                def turn_probs():
                    for c in range(2):
                        pe.wait_ge(probs_ready, it * 2 + (c + 1))
                        for n in (1, 2, 3, 0):
                            w = CHUNK if n == 0 else 2 * CHUNK
                            last = pe.transpose(ps[0:w, 6 + c, n * P:n * P + P], probs[c][:, n, 0:w], ident[:, :])
                        last.then_inc(probs_turned, 1)

                def weigh_values():
                    for c in range(2):
                        pe.wait_ge(probs_copied, it * 2 + (c + 1))
                        for n in (1, 2, 3, 0):
                            for h in range(2):
                                w = CHUNK if n == 0 else 2 * CHUNK
                                last = mm(ps[64 * h:64 * h + 64, 4 + c, n * CHUNK:n * CHUNK + CHUNK],
                                          v_st[0:w, [0, 0, 2, 1][n], :], probs_t[c][0:w, n, 64 * h:64 * h + 64],
                                          start=True, stop=True)
                    last.then_inc(att_ready, 1)

                def level(i):
                    if i == 0:
                        pe.wait_ge(gates_ready, it * 2 + 2)
                        pe.wait_ge(att_mixed, it + 1)
                    else:
                        pe.wait_ge(level_ready, it * 8 + i)
                    if i >= 4:
                        pe.wait_ge(level_taken, it * TAKES + (i - 3))
                    for n in range(4):
                        sl = slice(n * P, n * P + P)
                        if i == 0:
                            last = mm(ps[:, 4, sl], KK[:, sl], QS[:, sl], start=True, stop=True)
                        else:
                            E = big[:, (i - 1) % 4, sl]
                            blocks = upper_halves(E, i - 1)
                            last = mm(ps[:, 4 + i % 4, n * P:n * P + P // 2].rearrange("p (b n) -> p b n", n=1 << (i - 1)),
                                      E, blocks, start=True, stop=True)
                    last.then_inc(level_done, 1)

                def wide_levels():
                    pe.wait_ge(level_ready, it * 8 + 8)
                    pe.wait_ge(level_taken, it * TAKES + 4)
                    E = big[:, 7 % 4, :]
                    for h in range(2):
                        mm(ps[:, 7, SEQ + h * P:SEQ + h * P + P], E[:, h * SEQ:h * SEQ + P],
                           E[:, h * SEQ + P:h * SEQ + SEQ], start=True, stop=True)
                    E = big[:, 6 % 4, :]
                    for n in range(4):
                        last = mm(ps[0:64, 7, n * 64:n * 64 + 64], E[:, n * P:n * P + 64],
                                  E[:, n * P + 64:n * P + P], start=True, stop=True)
                    last.then_inc(level_done, 1)

                def weigh_inputs():
                    pe.wait_ge(cross_copied, it + 1)
                    pe.wait_ge(acc_free, g + 3)
                    for h in range(2):
                        hs = slice(h * P, h * P + P)
                        mm(ps[:, 7, h * SEQ:h * SEQ + P], i_nat[:, 0, hs], s_t[:, 2 * h, :], start=True, stop=True)
                        mm(ps[:, 7, h * SEQ + P:h * SEQ + SEQ], i_nat[:, 0, hs], s_x[:, h, :], start=True, stop=False)
                        last = mm(ps[:, 7, h * SEQ + P:h * SEQ + SEQ], i_nat[:, 1, hs], s_t[:, 2 * h + 1, :], start=False, stop=True)
                    last.then_inc(o_ready, 1)

                unit(g, 0, 0, act_in)
                unit(g, 0, 1, act_in)
                pe.wait_ge(staged, it + 1)
                unit(g, 0, 2, act_in)
                scores()
                pe.wait_ge(normed_ready, UNITS)
                unit(g, 0, 3, act_in)

                unit(g + 1, 1, 0, act_in)
                unit(g + 1, 1, 1, act_in)
                turn_probs()
                unit(g + 1, 1, 2, act_in)
                unit(g + 1, 1, 3, act_in)
                weigh_values()

                unit(g + 2, 0, 0, act_in, natural=True)
                unit(g + 2, 0, 1, act_in, natural=True)
                level(0)
                level(1)
                unit(g + 2, 0, 2, act_in, natural=True)
                level(2)
                level(3)
                unit(g + 2, 0, 3, act_in, natural=True)
                level(4)
                level(5)

                unit(g + 3, 1, 0, act_in)
                level(6)
                wide_levels()
                unit(g + 3, 1, 1, act_in)
                weigh_inputs()
                unit(g + 3, 1, 2, act_in)
                pe.wait_ge(osq_ready, it + 1)
                for n in range(4):
                    last = mm(ps[:, 6, n:n + 1], big[:, 0, n * P:n * P + P], ones[:, 0:1], start=True, stop=True)
                last.then_inc(oms_ready, 1)
                unit(g + 3, 1, 3, act_in)
                pe.wait_ge(odiag_ready, it + 1)
                mm(ps[:, 6, :], ones[:, :], big[:, 1, :], start=True, stop=True).then_inc(orstd_spread, 1)

            with pe.Fori(0, N_GROUPS // 2) as it:
                for j in range(2):
                    for u in range(UNITS):
                        if u < 2:
                            pe.wait_ge(att_mixed, 2 * u + 2)
                        else:
                            pe.wait_ge(hg_mixed, 2 * u - 2)
                        unit(it * 2 + (G_OUT + j), j, u, act_mid)

            for j in range(2):
                for u in range(UNITS):
                    pe.wait_ge(v_ready, 2 * u + 2)
                    unit(G_MLP + j, j, u, act_in)
                    if j == 0 and u == 1:
                        pe.wait_ge(sq_summed, N_GROUPS)
                        mm(ps[:, 4, 0:SEQ], ones[:, :], sq_acc[:, 0, :], start=True, stop=False)
                        mm(ps[:, 4, 0:SEQ], ones[:, :], sq_acc[:, 1, :], start=False, stop=True).then_inc(ms_ready, 1)

            def up(g0, first=0):
                with pe.Fori(first, N_GROUPS // 2) as it:
                    for j in range(2):
                        for u in range(UNITS):
                            pe.wait_ge(v_ready, 2 * u + 2)
                            unit(it * 2 + g0 + j, j, u, act_in)

            def down(c):
                with pe.Fori(0, N_GROUPS // 2) as it:
                    for j in range(2):
                        for u in range(UNITS):
                            pe.wait_ge(hid_ready, c * N_GROUPS + (2 * u + 2))
                            unit(it * 2 + c * (2 * N_GROUPS) + (G_MLP + N_GROUPS + j), j, u, act_mid)

            up(G_MLP, first=1)
            down(0)
            with pe.Fori(1, CHUNKS - 1) as c:
                up(c * (2 * N_GROUPS) + G_MLP)
                down(c)
            up(G_END - 2 * N_GROUPS)

            def turn_y(b, ready):
                pe.wait_ge(fin_gained, ready)
                for st in range(2):
                    for t in range(2):
                        last = pe.transpose(ps[:, b, st * SEQ + t * P:st * SEQ + t * P + P],
                                            relu_b[b - 4][:, t, st * P:st * P + P], ident[:, :])
                last.then_inc(y_turned, 1)

            def last_down(it, j):
                for u in range(UNITS):
                    pe.wait_ge(hid_ready, (CHUNKS - 1) * N_GROUPS + 2 * u + 2)
                    unit(it * 2 + (G_END - N_GROUPS + j), j, u, act_mid)
                    if u == 2 and not is_group(it, j, 0):
                        turn_y(5 - j, it * 2 + j)

            for it, j in FIRST_PAIR:
                last_down(it, j)
            with pe.Fori(1, N_GROUPS // 2 - 1) as it:
                for j in range(2):
                    last_down(it, j)
            last_down(*LAST_EVEN)

            def sum_squares(sq, a, first=False, end=False):
                for st in range(2):
                    last = mm(ps[:, 6 + st, 0:1], sq[:, a, st * P:st * P + P], ones[:, 0:1], start=first, stop=end)
                return last

            g = G_END - 1
            pe.wait_ge(acc_free, g - 1)
            for b in range(2):
                part = slice(b * P, b * P + P)
                to = ps[:, 2 + b, 0:SEQ]
                for u in range(UNITS):
                    pe.wait_ge(hid_ready, (CHUNKS - 1) * N_GROUPS + 2 * u + 2)
                    pe.wait_ge(lo_ready, g * UNITS + (u + 1))
                    for t in range(UK):
                        kt = UK * u + t
                        hi, lo = w_hi[:, UNITS + u, t, part], w_lo[:, UNITS + u, t, part]
                        mm(to, hi, act_mid[:, kt, 0:SEQ], start=kt == 0, stop=False)
                        mm(to, lo, act_mid[:, kt, 0:SEQ], start=False, stop=False)
                        last = mm(to, hi, act_mid[:, kt, SEQ:2 * SEQ], start=False, stop=kt == KT - 1)
                    if b == 0 and u == 2:
                        turn_y(4, N_GROUPS - 1)
                    if b == 1 and u == 0:
                        pe.wait_ge(sq_cleared, N_GROUPS)
                        sum_squares(sq_acc, 0, first=True)
                        sum_squares(sq_acc, 1)
                    if b == 1 and u == 2:
                        pe.wait_ge(fin_sq, N_GROUPS)
                        sum_squares(sq_b[1], 0)
                last.then_inc(tile_done, 1)
            pe.wait_ge(fin_gained, N_GROUPS)
            for st in range(2):
                pe.transpose(ps[:, 5, st * SEQ:st * SEQ + P], relu_b[1][:, 0, st * P:st * P + P], ident[:, :])
            pe.wait_ge(fin_sq, N_GROUPS + 1)
            sum_squares(sq_b[1], 1, end=True).then_inc(fms_ready, 1)
            pe.wait_ge(fin_gained, N_GROUPS + 1)
            for st in range(2):
                last = pe.transpose(ps[:, 5, st * SEQ + P:st * SEQ + SEQ], relu_b[1][:, 1, st * P:st * P + P], ident[:, :])
            last.then_inc(y_turned, 1)



def kernel(**inputs):
    import numpy as np
    import concourse.bacc as bacc
    from concourse.bass_utils import run_bass_kernel_spmd

    s, t = np.arange(P)[:, None], np.arange(P)[None, :]
    masks = [s == t] + [(s >> n == t >> n) & ((s >> (n - 1)) % 2 == 0) & ((t >> (n - 1)) % 2 == 1) for n in range(1, TAKES)]
    arrays = {name: np.ascontiguousarray(inputs[name]) for name in (
        "x", "norm_mix", "w_in", "attn_sinks", "lb_logits", "hgrn_norm", "w_out", "norm_mlp",
        "w_up", "w_down", "final_norm")}
    arrays["identity"] = np.eye(P, dtype=np.float32)
    arrays["level_masks"] = np.stack(masks, axis=1).astype(np.float32)

    nc = bacc.Bacc("TRN2", target_bir_lowering=False, num_devices=1)
    args = [nc.dram_tensor(f"in_{name}", a.shape, mybir.dt.from_np(a.dtype), kind="ExternalInput").ap()
            for name, a in arrays.items()]
    out = nc.dram_tensor("out_h", (1, SEQ, D_MODEL), F32, kind="ExternalOutput").ap()
    build(nc, *args, out)
    r = run_bass_kernel_spmd(nc, [{f"in_{name}": a for name, a in arrays.items()}], core_ids=[0])
    return r.results[0]["out_h"]
```
